# Optimizing a Trainium2 kernel written in Bass

```python
import jax, jax.numpy as jnp
from jax import lax
import numpy as np

D_MODEL = 1024
BATCH = 1
SEQ = 256
DEPTH = 2

N_MEM = 256
D_MIX = D_MODEL
CONV_HEADS = 4
CONV_DIM = D_MIX // 4
CONV_WIDTH = 3
REC_HEADS = 4
REC_DIM = D_MIX // 2
REC_HEAD_DIM = REC_DIM // REC_HEADS
REC_EXPAND = 128
REC_FDIM = REC_HEADS * REC_EXPAND
CHUNK = 64
POOL_DIM = D_MIX - CONV_DIM - REC_DIM
POOL_WINDOWS = (2, 4, 8, 16)
POOL_GROUP = POOL_DIM // len(POOL_WINDOWS)
D_IN = 3 * CONV_DIM + 2 * REC_FDIM + 2 * REC_DIM + POOL_DIM
CA_HEADS = 4
CA_HEAD_DIM = D_MODEL // CA_HEADS
D_FF = 2816
ALPHA = (2.0 * DEPTH) ** 0.25
BETA = (8.0 * DEPTH) ** -0.25
LN_EPS = 1e-5
RMS_EPS = 1e-6


def layer_norm(x, g, b):
    xf = x.astype(jnp.float32)
    mu = jnp.mean(xf, axis=-1, keepdims=True)
    var = jnp.mean(jnp.square(xf - mu), axis=-1, keepdims=True)
    return ((xf - mu) * lax.rsqrt(var + LN_EPS)).astype(x.dtype) * g + b

def swiglu(x, w_gate, w_up, w_down):
    return (jax.nn.silu(x @ w_gate) * (x @ w_up)) @ w_down

def short_gated_conv(h, b_gate, c_gate, w):
    u = c_gate * h
    s = u.shape[1]
    up = jnp.pad(u, ((0, 0), (CONV_WIDTH - 1, 0), (0, 0)))
    y = sum(w[k] * up[:, k:k + s] for k in range(CONV_WIDTH))
    return b_gate * y

def hgrn2(q, f_logit, v, g, lb, norm_g):
    bsz, s, _ = q.shape
    n_chunks = s // CHUNK
    f32 = jnp.float32
    f = lb + (1.0 - lb) * jax.nn.sigmoid(f_logit.astype(f32))
    logf = jnp.log(f)
    k = 1.0 - f

    def to_chunks(t, d):
        return t.reshape(bsz, n_chunks, CHUNK, REC_HEADS, d).transpose(1, 0, 3, 2, 4)

    qc = to_chunks(q.astype(f32), REC_EXPAND)
    kc = to_chunks(k, REC_EXPAND)
    lc = to_chunks(logf, REC_EXPAND)
    vc = to_chunks(v.astype(f32), REC_HEAD_DIM)
    mask = jnp.tril(jnp.ones((CHUNK, CHUNK), dtype=bool))

    def step(state, inp):
        qb, kb, vb, lb_ = inp
        b = jnp.cumsum(lb_, axis=2)
        diff = b[:, :, :, None, :] - b[:, :, None, :, :]
        decay = jnp.exp(jnp.where(mask[:, :, None], diff, -jnp.inf))
        attn = jnp.einsum('bhtd,bhsd,bhtsd->bhts', qb, kb, decay)
        o = (jnp.einsum('bhts,bhsv->bhtv', attn, vb)
             + jnp.einsum('bhtd,bhdv->bhtv', qb * jnp.exp(b), state))
        b_last = b[:, :, -1:, :]
        new_state = (jnp.exp(b_last[:, :, 0, :])[..., None] * state
                     + jnp.einsum('bhsd,bhsv->bhdv', kb * jnp.exp(b_last - b), vb))
        return new_state, o

    s0 = jnp.zeros((bsz, REC_HEADS, REC_EXPAND, REC_HEAD_DIM), f32)
    _, o = lax.scan(step, s0, (qc, kc, vc, lc))
    o = o.transpose(1, 0, 3, 2, 4).reshape(bsz, s, REC_HEADS, REC_HEAD_DIM)
    o = o * lax.rsqrt(jnp.mean(jnp.square(o), axis=-1, keepdims=True) + RMS_EPS)
    o = o * norm_g.reshape(REC_HEADS, REC_HEAD_DIM).astype(f32)
    o = o.reshape(bsz, s, REC_DIM) * jax.nn.sigmoid(g.astype(f32))
    return o.astype(v.dtype)

def multiscale_pool(u, w_pool, scale):
    bsz, s, _ = u.shape
    uf = u.astype(jnp.float32)
    cs = jnp.cumsum(uf, axis=1)
    t = jnp.arange(s)
    groups = []
    for gi, w in enumerate(POOL_WINDOWS):
        sl = slice(gi * POOL_GROUP, (gi + 1) * POOL_GROUP)
        c = cs[:, :, sl]
        win_sum = c - jnp.pad(c, ((0, 0), (w, 0), (0, 0)))[:, :s]
        count = jnp.minimum(t + 1, w).astype(jnp.float32)[None, :, None]
        groups.append(win_sum / count - uf[:, :, sl])
    p = jnp.stack(groups, axis=2).astype(u.dtype)
    y = jnp.einsum('bsgc,gcd->bsgd', p, w_pool).reshape(bsz, s, POOL_DIM)
    return y * scale

def cross_attn(x, mem, wq, wk, wv, wo):
    bsz, s, _ = x.shape
    m = mem.shape[1]
    q = (x @ wq).reshape(bsz, s, CA_HEADS, CA_HEAD_DIM)
    k = (mem @ wk).reshape(bsz, m, CA_HEADS, CA_HEAD_DIM)
    v = (mem @ wv).reshape(bsz, m, CA_HEADS, CA_HEAD_DIM)
    sc = jnp.einsum('bshd,bmhd->bhsm', q, k).astype(jnp.float32) * (CA_HEAD_DIM ** -0.5)
    p = jax.nn.softmax(sc, axis=-1).astype(v.dtype)
    o = jnp.einsum('bhsm,bmhd->bshd', p, v).reshape(bsz, s, D_MODEL)
    return o @ wo

def first_inputs(seed: int = 0) -> dict:
    key = jax.random.key(seed)
    ks = jax.random.split(key, 24)
    f32 = jnp.float32
    nrm = lambda k, shp, sc: jax.random.normal(k, shp, f32) * sc
    return {
        'x': nrm(ks[0], (BATCH, SEQ, D_MODEL), 1.0),
        'mem': nrm(ks[1], (BATCH, N_MEM, D_MODEL), 1.0),
        'ffn1_gate': nrm(ks[2], (DEPTH, D_MODEL, D_FF), BETA * D_MODEL ** -0.5),
        'ffn1_up': nrm(ks[3], (DEPTH, D_MODEL, D_FF), BETA * D_MODEL ** -0.5),
        'ffn1_down': nrm(ks[4], (DEPTH, D_FF, D_MODEL), BETA * D_FF ** -0.5),
        'w_in': nrm(ks[5], (DEPTH, D_MODEL, D_IN), D_MODEL ** -0.5),
        'conv_w': nrm(ks[6], (DEPTH, CONV_WIDTH, CONV_DIM), CONV_WIDTH ** -0.5),
        'rec_lb': nrm(ks[7], (DEPTH, REC_FDIM), 0.5),
        'rec_norm_g': 1.0 + nrm(ks[8], (DEPTH, REC_DIM), 0.02),
        'pool_w': nrm(ks[9], (DEPTH, len(POOL_WINDOWS), POOL_GROUP, POOL_GROUP), POOL_GROUP ** -0.5),
        'pool_scale': 1.0 + nrm(ks[10], (DEPTH, POOL_DIM), 0.02),
        'w_out': nrm(ks[11], (DEPTH, D_MIX, D_MODEL), BETA * D_MIX ** -0.5),
        'ca_q': nrm(ks[12], (DEPTH, D_MODEL, D_MODEL), D_MODEL ** -0.5),
        'ca_k': nrm(ks[13], (DEPTH, D_MODEL, D_MODEL), D_MODEL ** -0.5),
        'ca_v': nrm(ks[14], (DEPTH, D_MODEL, D_MODEL), BETA * D_MODEL ** -0.5),
        'ca_o': nrm(ks[15], (DEPTH, D_MODEL, D_MODEL), BETA * D_MODEL ** -0.5),
        'ffn2_gate': nrm(ks[16], (DEPTH, D_MODEL, D_FF), BETA * D_MODEL ** -0.5),
        'ffn2_up': nrm(ks[17], (DEPTH, D_MODEL, D_FF), BETA * D_MODEL ** -0.5),
        'ffn2_down': nrm(ks[18], (DEPTH, D_FF, D_MODEL), BETA * D_FF ** -0.5),
        'ln_g': 1.0 + nrm(ks[19], (DEPTH, 4, D_MODEL), 0.02),
        'ln_b': nrm(ks[20], (DEPTH, 4, D_MODEL), 0.02),
    }

def first_block(x, mem, ffn1_gate, ffn1_up, ffn1_down, w_in, conv_w, rec_lb, rec_norm_g,
              pool_w, pool_scale, w_out, ca_q, ca_k, ca_v, ca_o,
              ffn2_gate, ffn2_up, ffn2_down, ln_g, ln_b):
    sm = jax.nn.softmax(rec_lb.astype(jnp.float32), axis=0)
    lbs = jnp.cumsum(sm, axis=0) - sm[0:1]
    split_at = np.cumsum([CONV_DIM, CONV_DIM, CONV_DIM, REC_FDIM, REC_FDIM, REC_DIM, REC_DIM])
    h = x
    for l in range(DEPTH):
        h = layer_norm(ALPHA * h + 0.5 * swiglu(h, ffn1_gate[l], ffn1_up[l], ffn1_down[l]),
                       ln_g[l, 0], ln_b[l, 0])
        z = h @ w_in[l]
        cb, cc, ch, rq, rf, ri, rg, pu = jnp.split(z, split_at, axis=-1)
        y_conv = short_gated_conv(ch, cb, cc, conv_w[l])
        y_rec = hgrn2(rq, rf, ri, rg, lbs[l], rec_norm_g[l])
        y_pool = multiscale_pool(pu, pool_w[l], pool_scale[l])
        mix = jnp.concatenate([y_conv, y_rec, y_pool], axis=-1) @ w_out[l]
        h = layer_norm(ALPHA * h + mix, ln_g[l, 1], ln_b[l, 1])
        h = layer_norm(ALPHA * h + cross_attn(h, mem, ca_q[l], ca_k[l], ca_v[l], ca_o[l]),
                       ln_g[l, 2], ln_b[l, 2])
        h = layer_norm(ALPHA * h + 0.5 * swiglu(h, ffn2_gate[l], ffn2_up[l], ffn2_down[l]),
                       ln_g[l, 3], ln_b[l, 3])
    return h


DEPTH_2 = 1

PLE_DIM = 256
LRU_WIDTH = D_MODEL
LRU_BLOCKS = 8
LRU_BLOCK = LRU_WIDTH // LRU_BLOCKS
CONV_WIDTH_2 = 4
LRU_C = 8.0
LRU_A_MIN = 0.9
LRU_A_MAX = 0.999
GLA_HEADS = 4
GLA_DK = D_MODEL // 2 // GLA_HEADS
GLA_DV = D_MODEL // GLA_HEADS
GLA_RANK = 16
GLA_TAU = 16.0
GLA_CHUNK = 64
N_EXPERTS = 32
TOP_K = 4
D_FF_2 = D_MODEL
SWIGLU_LIMIT = 7.0
SWIGLU_ALPHA = 1.702
MOE_BLOCK = 128
RMS_EPS_2 = 1e-5
DEEPNORM_ALPHA = (2.0 * DEPTH_2) ** 0.25
DEEPNORM_BETA = (8.0 * DEPTH_2) ** -0.25

IN_WIDTHS = [LRU_WIDTH, LRU_WIDTH, GLA_HEADS * GLA_DK, GLA_HEADS * GLA_DK,
             GLA_HEADS * GLA_DV, GLA_HEADS * GLA_DV, GLA_RANK, D_MODEL, D_MODEL]
IN_TOTAL = int(sum(IN_WIDTHS))
IN_SPLITS = [int(s) for s in np.cumsum(IN_WIDTHS)[:-1]]


def layer_norm_2(x, g, b):
    xf = x.astype(jnp.float32)
    mu = jnp.mean(xf, axis=-1, keepdims=True)
    var = jnp.mean(jnp.square(xf - mu), axis=-1, keepdims=True)
    return ((xf - mu) * lax.rsqrt(var + LN_EPS) * g + b).astype(x.dtype)

def causal_depthwise_conv(x, w, b):
    s = x.shape[1]
    xp = jnp.pad(x, ((0, 0), (CONV_WIDTH_2 - 1, 0), (0, 0)))
    out = xp[:, 0:s] * w[0]
    for k in range(1, CONV_WIDTH_2):
        out = out + xp[:, k:k + s] * w[k]
    return out + b

def rg_lru(x, w_r, b_r, w_i, b_i, lam):
    bsz, s, c = x.shape
    xb = x.reshape(bsz, s, LRU_BLOCKS, LRU_BLOCK)
    r = jax.nn.sigmoid(jnp.einsum('bsgc,gcd->bsgd', xb, w_r).reshape(bsz, s, c) + b_r)
    i = jax.nn.sigmoid(jnp.einsum('bsgc,gcd->bsgd', xb, w_i).reshape(bsz, s, c) + b_i)
    log_a = (-LRU_C * r * jax.nn.softplus(-lam)).astype(jnp.float32)
    a = jnp.exp(log_a)
    mult = jnp.sqrt(-jnp.expm1(2.0 * log_a))
    u = mult * (i * x).astype(jnp.float32)

    def combine(left, right):
        a1, b1 = left
        a2, b2 = right
        return a1 * a2, a2 * b1 + b2

    _, h = lax.associative_scan(combine, (a, u), axis=1)
    return h.astype(x.dtype)

def gla_chunked(q, k, v, log_g):
    bsz, s, h, dk = q.shape
    dv = v.shape[-1]
    n = s // GLA_CHUNK

    def to_chunks(t):
        t = t.astype(jnp.float32).reshape(bsz, n, GLA_CHUNK, h, t.shape[-1])
        return t.transpose(1, 0, 3, 2, 4)

    qc = to_chunks(q * (dk ** -0.5))
    kc, vc, gc = to_chunks(k), to_chunks(v), to_chunks(log_g)
    causal = jnp.tril(jnp.ones((GLA_CHUNK, GLA_CHUNK), dtype=bool))

    def step(state, inp):
        qn, kn, vn, gn = inp
        bcum = jnp.cumsum(gn, axis=2)
        o_inter = jnp.einsum('bhik,bhkv->bhiv', qn * jnp.exp(bcum), state)
        diff = bcum[:, :, :, None, :] - bcum[:, :, None, :, :]
        decay = jnp.exp(jnp.where(causal[:, :, None], diff, -jnp.inf))
        scores = jnp.einsum('bhijk,bhjk->bhij', qn[:, :, :, None, :] * decay, kn)
        o_intra = jnp.einsum('bhij,bhjv->bhiv', scores, vn)
        b_last = bcum[:, :, -1:, :]
        k_dec = kn * jnp.exp(b_last - bcum)
        state = (jnp.exp(b_last[:, :, 0, :])[..., None] * state
                 + jnp.einsum('bhjk,bhjv->bhkv', k_dec, vn))
        return state, o_inter + o_intra

    state0 = jnp.zeros((bsz, h, dk, dv), jnp.float32)
    _, o = lax.scan(step, state0, (qc, kc, vc, gc))
    o = o.transpose(1, 0, 3, 2, 4).reshape(bsz, s, h, dv)
    return o

def moe(x, w_router, b_router, w_up, b_up, w_down, b_down):
    bsz, s, d = x.shape
    t = bsz * s
    xt = x.reshape(t, d)
    logits = (xt @ w_router + b_router).astype(jnp.float32)
    top_val, top_idx = lax.top_k(logits, TOP_K)
    gates = jax.nn.softmax(top_val, axis=-1).astype(x.dtype)

    n_assign = t * TOP_K
    expert_flat = top_idx.reshape(n_assign)
    token_flat = (jnp.arange(n_assign, dtype=jnp.int32) // TOP_K).astype(jnp.int32)
    gate_flat = gates.reshape(n_assign)
    order = jnp.argsort(expert_flat)
    sorted_expert = expert_flat[order]
    counts = jnp.bincount(expert_flat, length=N_EXPERTS)
    start = jnp.cumsum(counts) - counts
    padded_counts = (counts + MOE_BLOCK - 1) // MOE_BLOCK * MOE_BLOCK
    padded_end = jnp.cumsum(padded_counts)
    padded_start = padded_end - padded_counts
    slot = padded_start[sorted_expert] + jnp.arange(n_assign) - start[sorted_expert]

    n_slots = n_assign + N_EXPERTS * MOE_BLOCK
    n_blocks = n_slots // MOE_BLOCK
    slot_token = jnp.full((n_slots,), t, jnp.int32).at[slot].set(token_flat[order])
    slot_gate = jnp.zeros((n_slots,), x.dtype).at[slot].set(gate_flat[order])
    block_expert = jnp.minimum(
        jnp.searchsorted(padded_end, jnp.arange(n_blocks) * MOE_BLOCK, side='right'),
        N_EXPERTS - 1)
    x_pad = jnp.concatenate([xt, jnp.zeros((1, d), xt.dtype)], axis=0)

    def expert_block(args):
        tok, g, e = args
        xb = x_pad[tok]
        hdn = xb @ w_up[e] + b_up[e]
        gate_h = jnp.minimum(hdn[:, :D_FF_2], SWIGLU_LIMIT)
        up_h = jnp.clip(hdn[:, D_FF_2:], -SWIGLU_LIMIT, SWIGLU_LIMIT)
        act = (up_h + 1.0) * gate_h * jax.nn.sigmoid(SWIGLU_ALPHA * gate_h)
        y = act @ w_down[e] + b_down[e]
        return y * g[:, None]

    y_slots = lax.map(expert_block, (slot_token.reshape(n_blocks, MOE_BLOCK),
                                     slot_gate.reshape(n_blocks, MOE_BLOCK),
                                     block_expert))
    out = jnp.zeros((t + 1, d), y_slots.dtype).at[slot_token].add(y_slots.reshape(n_slots, d))
    return out[:t].reshape(bsz, s, d)

def second_inputs(seed: int = 0) -> dict:
    key = jax.random.key(seed)
    ks = jax.random.split(key, 27)
    f32 = jnp.float32
    L = DEPTH_2

    def nrm(k, shape, scale):
        return jax.random.normal(k, shape, f32) * scale

    u = jax.random.uniform(ks[9], (L, LRU_WIDTH), f32, LRU_A_MIN, LRU_A_MAX)
    s_base = u ** (1.0 / LRU_C)
    lru_lambda = jnp.log(s_base) - jnp.log1p(-s_base)
    return {
        "x": nrm(ks[0], (BATCH, SEQ, D_MODEL), 1.0),
        "p": nrm(ks[1], (DEPTH_2, BATCH, SEQ, PLE_DIM), 1.0),
        "w_in": nrm(ks[2], (L, D_MODEL, IN_TOTAL), D_MODEL ** -0.5),
        "conv_w": nrm(ks[3], (L, CONV_WIDTH_2, LRU_WIDTH), CONV_WIDTH_2 ** -0.5),
        "conv_b": nrm(ks[4], (L, LRU_WIDTH), 0.01),
        "lru_w_r": nrm(ks[5], (L, LRU_BLOCKS, LRU_BLOCK, LRU_BLOCK), LRU_BLOCK ** -0.5),
        "lru_b_r": nrm(ks[6], (L, LRU_WIDTH), 0.01),
        "lru_w_i": nrm(ks[7], (L, LRU_BLOCKS, LRU_BLOCK, LRU_BLOCK), LRU_BLOCK ** -0.5),
        "lru_b_i": nrm(ks[8], (L, LRU_WIDTH), 0.01),
        "lru_lambda": lru_lambda,
        "gla_w_gate": nrm(ks[10], (L, GLA_RANK, GLA_HEADS * GLA_DK), GLA_RANK ** -0.5),
        "gla_b_gate": nrm(ks[11], (L, GLA_HEADS * GLA_DK), 0.01),
        "gla_norm_g": 1.0 + nrm(ks[12], (L, GLA_DV), 0.02),
        "w_out": nrm(ks[13], (L, D_MODEL, D_MODEL), DEEPNORM_BETA * D_MODEL ** -0.5),
        "ln1_g": 1.0 + nrm(ks[14], (L, D_MODEL), 0.02),
        "ln1_b": nrm(ks[15], (L, D_MODEL), 0.01),
        "w_router": nrm(ks[16], (L, D_MODEL, N_EXPERTS), D_MODEL ** -0.5),
        "b_router": nrm(ks[17], (L, N_EXPERTS), 0.01),
        "w_up": nrm(ks[18], (L, N_EXPERTS, D_MODEL, 2 * D_FF_2), D_MODEL ** -0.5),
        "b_up": nrm(ks[19], (L, N_EXPERTS, 2 * D_FF_2), 0.01),
        "w_down": nrm(ks[20], (L, N_EXPERTS, D_FF_2, D_MODEL), DEEPNORM_BETA * D_FF_2 ** -0.5),
        "b_down": nrm(ks[21], (L, N_EXPERTS, D_MODEL), 0.01),
        "ln2_g": 1.0 + nrm(ks[22], (L, D_MODEL), 0.02),
        "ln2_b": nrm(ks[23], (L, D_MODEL), 0.01),
        "w_ple": nrm(ks[24], (L, PLE_DIM, D_MODEL), PLE_DIM ** -0.5),
        "w_ple_gate": nrm(ks[25], (L, D_MODEL, D_MODEL), D_MODEL ** -0.5),
        "b_ple_gate": nrm(ks[26], (L, D_MODEL), 0.01),
    }

def second_block(x, p, w_in, conv_w, conv_b, lru_w_r, lru_b_r, lru_w_i, lru_b_i, lru_lambda,
              gla_w_gate, gla_b_gate, gla_norm_g, w_out, ln1_g, ln1_b,
              w_router, b_router, w_up, b_up, w_down, b_down, ln2_g, ln2_b,
              w_ple, w_ple_gate, b_ple_gate):
    bsz, s, d = x.shape
    h = x
    for i in range(DEPTH_2):
        proj = h @ w_in[i]
        xa, ga, q, k, v, go, glr, ma, mb = jnp.split(proj, IN_SPLITS, axis=-1)

        xa = causal_depthwise_conv(xa, conv_w[i], conv_b[i])
        ya = rg_lru(xa, lru_w_r[i], lru_b_r[i], lru_w_i[i], lru_b_i[i], lru_lambda[i])
        ya = ya * jax.nn.gelu(ga)

        log_g = jax.nn.log_sigmoid(glr @ gla_w_gate[i] + gla_b_gate[i]) / GLA_TAU
        o = gla_chunked(q.reshape(bsz, s, GLA_HEADS, GLA_DK),
                        k.reshape(bsz, s, GLA_HEADS, GLA_DK),
                        v.reshape(bsz, s, GLA_HEADS, GLA_DV),
                        log_g.reshape(bsz, s, GLA_HEADS, GLA_DK))
        o = o * lax.rsqrt(jnp.mean(jnp.square(o), axis=-1, keepdims=True) + RMS_EPS_2) * gla_norm_g[i]
        yb = o.reshape(bsz, s, GLA_HEADS * GLA_DV).astype(h.dtype) * jax.nn.silu(go)

        y = jax.nn.sigmoid(ma) * ya + jax.nn.sigmoid(mb) * yb
        h = layer_norm_2(DEEPNORM_ALPHA * h + y @ w_out[i], ln1_g[i], ln1_b[i])

        m = moe(h, w_router[i], b_router[i], w_up[i], b_up[i], w_down[i], b_down[i])
        h = layer_norm_2(DEEPNORM_ALPHA * h + m, ln2_g[i], ln2_b[i])

        h = h + jax.nn.sigmoid(h @ w_ple_gate[i] + b_ple_gate[i]) * (p[i] @ w_ple[i])
    return h


_first_inputs = second_inputs


def second_inputs(seed=0):
    import zlib

    import numpy as np

    out = dict(_first_inputs(seed))
    spreads = {}
    factors = {'conv_b': 4.443,
     'lru_b_r': 182.534,
     'lru_b_i': 124.051,
     'gla_b_gate': 8.0,
     'gla_norm_g': 6.054,
     'ln1_b': 3.182,
     'b_router': 4.893,
     'b_up': 8.0,
     'b_down': 8.0,
     'ln2_g': 25.171,
     'ln2_b': 51.969,
     'b_ple_gate': 200.0}
    for name, (base, spread) in spreads.items():
        noise = np.random.default_rng([zlib.crc32(name.encode()), seed]).standard_normal(out[name].shape)
        drawn = base * np.exp(spread * noise) if base else spread * noise
        out[name] = __import__('jax').numpy.asarray(drawn.astype(out[name].dtype))
    for name, factor in factors.items():
        out[name] = (out[name] * factor).astype(out[name].dtype)
    return out


def setup_inputs(seed=0):
    out = dict(first_inputs(seed))
    for name, value in second_inputs(seed + 1).items():
        if name != "x":
            out[name + "_2"] = value
    return out


def reference(
    x, mem, ffn1_gate, ffn1_up, ffn1_down, w_in, conv_w, rec_lb, rec_norm_g, pool_w, pool_scale,
    w_out, ca_q, ca_k, ca_v, ca_o, ffn2_gate, ffn2_up, ffn2_down, ln_g, ln_b, p_2, w_in_2,
    conv_w_2, conv_b_2, lru_w_r_2, lru_b_r_2, lru_w_i_2, lru_b_i_2, lru_lambda_2, gla_w_gate_2,
    gla_b_gate_2, gla_norm_g_2, w_out_2, ln1_g_2, ln1_b_2, w_router_2, b_router_2, w_up_2,
    b_up_2, w_down_2, b_down_2, ln2_g_2, ln2_b_2, w_ple_2, w_ple_gate_2, b_ple_gate_2,
):
    x = first_block(
        x, mem, ffn1_gate, ffn1_up, ffn1_down, w_in, conv_w, rec_lb, rec_norm_g, pool_w,
        pool_scale, w_out, ca_q, ca_k, ca_v, ca_o, ffn2_gate, ffn2_up, ffn2_down, ln_g, ln_b,
    )
    return second_block(
        x, p_2, w_in_2, conv_w_2, conv_b_2, lru_w_r_2, lru_b_r_2, lru_w_i_2, lru_b_i_2,
        lru_lambda_2, gla_w_gate_2, gla_b_gate_2, gla_norm_g_2, w_out_2, ln1_g_2, ln1_b_2,
        w_router_2, b_router_2, w_up_2, b_up_2, w_down_2, b_down_2, ln2_g_2, ln2_b_2, w_ple_2,
        w_ple_gate_2, b_ple_gate_2,
    )


_drawn_inputs = setup_inputs


def setup_inputs(seed=0):
    import zlib

    import numpy as np

    out = dict(_drawn_inputs(seed))
    spreads = {}
    factors = {'rec_norm_g': 4.74,
     'pool_scale': 3.691,
     'ln2_g_2': 8.66,
     'ln2_b_2': 8.146,
     'w_ple_gate_2': 23.656,
     'b_ple_gate_2': 200.0,
     'p_2': 5.97,
     'w_ple_2': 5.932}
    for name, (base, spread) in spreads.items():
        noise = np.random.default_rng([zlib.crc32(name.encode()), seed]).standard_normal(out[name].shape)
        drawn = base * np.exp(spread * noise) if base else spread * noise
        out[name] = __import__('jax').numpy.asarray(drawn.astype(out[name].dtype))
    for name, factor in factors.items():
        out[name] = (out[name] * factor).astype(out[name].dtype)
    return out
```

```python
from contextlib import ExitStack, contextmanager

import numpy as np
import concourse.bass as bass
from concourse import mybir

F32 = mybir.dt.float32
U8 = mybir.dt.uint8
ALU = mybir.AluOpType
ACT = mybir.ActivationFunctionType
AX = mybir.AxisListType

P = 128
T = 256
TT = T // P
D = 1024
DT = D // P
LAYERS = 2
FF = 2816
CH = 256
NCH = FF // CH
RING = 12
SLOT = 2048
ALPHA = (2.0 * LAYERS) ** 0.25
ALPHA2 = 2.0 ** 0.25
LN_EPS = 1e-5
HEADS = 4
LEVELS = 9
EXPERTS = 32
TOPK = 4
LIMIT = 7.0
SIG_ALPHA = 1.702

COLS1 = [("ln_g", 64), ("ln_b", 64)]
COLS2 = [("rec_lb", 8), ("rec_norm_g", 8), ("conv_w", 12), ("pool_scale", 4), ("conv_w_2", 32),
         ("conv_b_2", 8), ("lru_b_r_2", 8), ("lru_b_i_2", 8), ("lru_lambda_2", 8),
         ("gla_b_gate_2", 4), ("gla_norm_g_2", 2)]
COLS3 = [("ln1_g_2", 8), ("ln1_b_2", 8), ("ln2_g_2", 8), ("ln2_b_2", 8)]

Q, K, PR, SU, FQ, FK, AA, AX_, V, Y = 0, 1024, 2048, 3072, 4096, 5120, 6144, 7168, 7680, 9728
MEMT, KT, VM, CC, UP = 11776, 13824, 15872, 17920, 18432
PU, SA, SB, PM, TC = 8704, 18948, 19492, 20036, 20548
XC, XA, R, IG, TH = 11776, 13824, 13824, 15904, 17952
WORK = 20804


class Book:

    def __init__(self):
        self.place, self.per = {}, {}
        self.old_place, self.old_per = None, None
        self.slots = {}
        self.iters = {}

    def turn(self):
        self.old_place, self.old_per = self.place, self.per
        self.place, self.per = {}, {}


class Line:

    def __init__(self, book, sem, key, unit=1):
        self.book, self.sem, self.key, self.unit = book, sem, key, unit
        self.n, self.loops = 0, []

    def add(self, name):
        self.n += 1
        assert (self.key, name) not in self.book.place, (self.key, name)
        self.book.place[self.key, name] = (self.n, tuple(self.loops))
        return self.sem

    def at(self, name, plus=0, **iters):
        if self.book.old_place is None:
            return 1
        n, loops = self.book.old_place[self.key, name]
        v = plus + n
        for loop in loops:
            per = self.book.old_per[self.key, loop]
            it = iters[loop] if loop in iters else self.book.iters[loop]
            if per and not (isinstance(it, int) and it == 0):
                v = v + it * per
        return v * self.unit


@contextmanager
def counted(book, eng, name, n, lines):
    start = [ln.n for ln in lines]
    for ln in lines:
        ln.loops.append(name)
    with eng.Fori(0, n) as it:
        book.iters[name] = it
        yield it
    del book.iters[name]
    for ln, s in zip(lines, start):
        ln.loops.pop()
        ln.book.per[ln.key, name] = ln.n - s
        ln.n = s + (ln.n - s) * n


def program(nc, book, a):
    book.iters = {}
    with ExitStack() as ctx:
        def sb(name, shape, dt=F32):
            return ctx.enter_context(nc.sbuf_tensor(name, shape, dt))

        def line(name, unit=1):
            return Line(book, ctx.enter_context(nc.semaphore(name)), name, unit)

        ring = sb("ring", [P, RING, SLOT])
        h = sb("h", [P, TT, D])
        hn = sb("hn", [P, TT, D])
        hT = sb("hT", [P, DT, T])
        work = sb("work", [P, WORK])
        ident = sb("ident", [P, P])
        ones = sb("ones", [P, P])
        mask = sb("mask", [P, 8, P], U8)
        cols = sb("cols", [P, 3, P])
        cnt = sb("cnt", [P, 2, 17])
        wpool = sb("wpool", [P, 2, P])
        lbt = sb("lbt", [P, 2, 8])
        sp8 = sb("sp8", [P, 2, 8])
        stat = sb("stat", [P, TT, 2, 6])
        mv = sb("mv", [P, TT, 2])
        rstd = sb("rstd", [P, TT])
        small = sb("small", [P, 64])
        taps = sb("taps", [P, 6])
        epsc = sb("epsc", [P, 3])
        smax = sb("smax", [P, HEADS, TT])
        ssum = sb("ssum", [P, HEADS, TT])
        brout = sb("brout", [1, 32])
        ps = ctx.enter_context(nc.psum_tensor("ps", [P, 8, 512], F32))

        loaded = [line(f"loaded{s}", 16) for s in range(RING)]
        used = [line(f"used{s}") for s in range(RING)]
        emptied = [line(f"emptied{b}") for b in range(8)]
        pe_full = line("pe_full")
        act_done = line("act_done")
        dve_done = line("dve_done")
        pool_done = line("pool_done")
        h_ready = line("h_ready")
        first = line("first_loads", 16)
        prm = line("param_loads", 16)
        out_done = line("out_done", 16)
        passed = ctx.enter_context(nc.semaphore("passed"))

        slot_of = book.slots

        def w(off, size, shape=None, **kw):
            v = work[:, off:off + size]
            return v.rearrange(shape, **kw) if shape else v

        qT = w(Q, 1024, "p (g t) -> p g t", g=4)
        kT_ = w(K, 1024, "p (g t) -> p g t", g=4)
        pr = w(PR, 1024, "p (g t) -> p g t", g=4)
        su = w(SU, 1024, "p (g t) -> p g t", g=4)
        fq = w(FQ, 1024)
        fk = w(FK, 1024)
        attn = w(AA, 1024, "p (t h s) -> p t h s", t=TT, h=HEADS)
        cross = w(AX_, 512, "p (h s) -> p h s", h=HEADS)
        yT = w(Y, 2048, "p (g t) -> p g t", g=8)
        memT = w(MEMT, 2048, "p (g t) -> p g t", g=8)
        keyT = w(KT, 2048, "p (g t) -> p g t", g=8)
        valm = w(VM, 2048, "p (t n) -> p t n", t=TT)

        def col(name, i, n=1):
            for b, group in enumerate((COLS1, COLS2, COLS3)):
                at = 0
                for nm, rows in group:
                    if nm == name:
                        if isinstance(i, int):
                            return cols[:, b, at + i:at + i + n]
                        return cols[:, b, bass.ds(i + at, n)]
                    at += rows

        def key(tag, what, c):
            return (tag, what, c)

        def obank(tag, j):
            return (2, 3)[j] if tag == "r" else (2, 3, 4, 5)[j]

        def slot_used(eng, name, plus=0, **iters):
            s = slot_of[name]
            eng.wait_ge(used[s].sem, used[s].at(name, plus + 1, **iters))

        def plain(eng):
            eng.sem_inc(passed, 1)

        block = ctx.enter_context(nc.Block())

        @block.sync
        def _(sp):
            def once(dst, src):
                sp.dma_start(dst, src).then_inc(first.add(first.n), 16)

            once(ident[:], a["c_ident"])
            once(h[:], a["x"].rearrange("a (t p) n -> p (a t) n", p=P))
            once(w(KT, 2048, "p (t n) -> p t n", t=TT), a["mem"].rearrange("a (t p) n -> p (a t) n", p=P))
            once(w(V, 1024), a["c_mask"].rearrange("p l t -> p (l t)"))
            once(cnt[:], a["c_cnt"])
            once(brout[:], a["b_router_2"])
            pos = [0]

            def load(name, src, shape, part=P, **kw):
                s = pos[0] % RING
                pos[0] += 1
                used[s].add(name)
                loaded[s].add(name)
                slot_of[name] = s
                n = 1
                for x in src.shape[1:]:
                    n *= x
                dst = ring[0:part, s, 0:n]
                if shape:
                    dst = dst.rearrange(shape, **kw)
                sp.wait_ge(used[s].sem, used[s].at(name))
                plain(sp)
                sp.dma_start(dst, src).then_inc(loaded[s].sem, 16)

            def align():
                pos[0] = -(-pos[0] // RING) * RING

            def columns(wt, c0):
                return wt.rearrange("(k p) n -> p k n", p=P)[:, :, c0:c0 + CH]

            def rows(wt, k0, n=2):
                return wt.rearrange("(k p) n -> p k n", p=P)[:, k0:k0 + n, :]

            def ln_params(name, g, b, i):
                s = pos[0] % RING
                pos[0] += 1
                used[s].add(name)
                loaded[s].add(name + ("g",))
                loaded[s].add(name)
                slot_of[name] = s
                sp.wait_ge(used[s].sem, used[s].at(name))
                plain(sp)
                for half, x in enumerate((g, b)):
                    sp.dma_start(ring[:, s, half * D:half * D + D],
                                 x[bass.ds(i, 1) if not isinstance(i, int) else slice(i, i + 1), :]
                                 .to_broadcast([P, D])).then_inc(loaded[s].sem, 16)

            def ffn(tag, wg, wu, wd, L):
                g = wg.rearrange("l (k p) n -> p l k n", p=P)
                u = wu.rearrange("l (k p) n -> p l k n", p=P)
                d = wd.rearrange("l (k p) n -> p l k n", p=P)

                def chunk(c, i=None):
                    n0 = bass.ds(i * (4 * CH) + c * CH, CH) if i is not None else slice(c * CH, c * CH + CH)
                    k0 = bass.ds(i * 8 + 2 * c, 2) if i is not None else slice(2 * c, 2 * c + 2)
                    load(key(tag, "gate", c), g[:, L, :, n0], "p (k n) -> p k n", k=DT)
                    load(key(tag, "up", c), u[:, L, :, n0], "p (k n) -> p k n", k=DT)
                    load(key(tag, "down", c), d[:, L, k0, :], "p (k n) -> p k n", k=2)

                chunk(0)
                chunk(1)
                with counted(book, sp, "c" + tag, 2, loaded + used) as i:
                    for c in range(2, 6):
                        chunk(c, i)
                pos[0] += 12
                chunk(10)

            with counted(book, sp, "L", LAYERS, loaded + used) as L:
                def wl(nm):
                    return a[nm].rearrange("l (k p) n -> p l k n", p=P)

                ffn("f1", a["ffn1_gate"], a["ffn1_up"], a["ffn1_down"], L)
                lng, lnb = (a[x].rearrange("l j n -> (l j) n") for x in ("ln_g", "ln_b"))
                ln_params(("lnp", 0), lng, lnb, L * 4)
                align()
                win = wl("w_in")

                def win_cols(name, c0):
                    load(name, win[:, L, :, c0:c0 + CH], "p (k n) -> p k n", k=DT)

                def full_cols(name, nm, c0):
                    load(name, wl(nm)[:, L, :, c0:c0 + CH], "p (k n) -> p k n", k=DT)

                def full_rows(name, nm, k0):
                    load(name, wl(nm)[:, L, k0:k0 + 2, :], "p (k n) -> p k n", k=2)

                for name, c0 in (("rf0", 1280), ("rf1", 1536), ("rq0", 768), ("rq1", 1024), ("cc", 256),
                                 ("ch", 512), ("cb", 0), ("pu", 2816)):
                    win_cols(name, c0)
                for j in range(2):
                    load(f"ri{j}", win[:, L, 4 * j:4 * j + 4, 1792:2304], "p (k n) -> p k n", k=4)
                for j in range(4):
                    full_cols(f"ck{j}", "ca_k", CH * j)
                for j in range(4):
                    full_rows(f"cv{j}", "ca_v", 2 * j)
                win_cols("rg0", 2304)
                win_cols("rg1", 2560)
                for j, k0 in enumerate((0, 6, 2, 4)):
                    full_rows(f"wo{j}", "w_out", k0)
                ln_params(("lnp", 1), lng, lnb, L * 4 + 1)
                for j in range(4):
                    full_cols(f"cq{j}", "ca_q", CH * j)
                for j in range(4):
                    full_rows(f"co{j}", "ca_o", 2 * j)
                ln_params(("lnp", 2), lng, lnb, L * 4 + 2)
                align()
                ffn("f2", a["ffn2_gate"], a["ffn2_up"], a["ffn2_down"], L)
                ln_params(("lnp", 3), lng, lnb, L * 4 + 3)
                align()

            win2 = a["w_in_2"].rearrange("a k n -> (a k) n")

            def cols2(name, c0):
                load(name, columns(win2, c0), "p (k n) -> p k n", k=DT)

            for j in range(4):
                cols2(f"xa{j}", CH * j)
            for j in range(2):
                cols2(f"q{j}", 2048 + CH * j)
            for j in range(2):
                cols2(f"k{j}", 2560 + CH * j)
            load("glr", win2.rearrange("(k p) n -> p k n", p=P)[:, :, 5120:5136], "p (k n) -> p k n", k=DT)
            load("glg", a["gla_w_gate_2"].rearrange("a r n -> (a r) n"), None, part=16)
            for j in range(4):
                load(f"v{j}", win2.rearrange("(k p) n -> p k n", p=P)[:, 2 * j:2 * j + 2, 3072:4096],
                     "p (k n) -> p k n", k=2)
            load("lrur", a["lru_w_r_2"].rearrange("a g c d -> c (a g) d"), "p (g d) -> p g d", g=8)
            load("lrui", a["lru_w_i_2"].rearrange("a g c d -> c (a g) d"), "p (g d) -> p g d", g=8)
            for j in range(4):
                cols2(f"go{j}", 4096 + CH * j)
            for j in range(4):
                cols2(f"mb{j}", 6160 + CH * j)
            for j in range(4):
                cols2(f"ga{j}", 1024 + CH * j)
            for j in range(4):
                cols2(f"ma{j}", 5136 + CH * j)
            wout2 = a["w_out_2"].rearrange("a k n -> (a k) n")
            for j in range(4):
                load(f"w2o{j}", rows(wout2, 2 * j), "p (k n) -> p k n", k=2)
            ln_params(("lnp", "A"), a["ln1_g_2"], a["ln1_b_2"], 0)
            load("router", a["w_router_2"].rearrange("a (k p) n -> p (a k) n", p=P), "p (k n) -> p k n", k=DT)
            load("tri", a["c_tri"], None)
            load("bup", a["b_up_2"].rearrange("a e (j n) -> (a e j) n", n=P)
                 .rearrange("(b p) n -> p b n", p=P), "p (b n) -> p b n", b=4)
            load("bdown", a["b_down_2"].rearrange("a e n -> (a e) n"), None, part=32)
            align()
            wup = a["w_up_2"].rearrange("a e (k p) n -> p (a e) k n", p=P)
            wdn = a["w_down_2"].rearrange("a e (k p) n -> p (a e) k n", p=P)
            with counted(book, sp, "e", EXPERTS, loaded + used) as e:
                for what, j in (("g", 0), ("u", 0), ("g", 1), ("u", 1), ("d", 0), ("g", 2), ("u", 2),
                                ("d", 1), ("g", 3), ("u", 3), ("d", 2), ("d", 3)):
                    if what == "d":
                        load(("moe", what, j), wdn[:, e, 2 * j:2 * j + 2, :], "p (k n) -> p k n", k=2)
                    else:
                        c0 = CH * j + (D if what == "u" else 0)
                        load(("moe", what, j), wup[:, e, :, c0:c0 + CH], "p (k n) -> p k n", k=DT)
            ln_params(("lnp", "B"), a["ln2_g_2"], a["ln2_b_2"], 0)
            load("ptok", a["p_2"].rearrange("l a (t p) n -> p (l a t) n", p=P), "p (t n) -> p t n", t=TT)
            load("wple", rows(a["w_ple_2"].rearrange("a k n -> (a k) n"), 0), "p (k n) -> p k n", k=2)
            load("bpg", a["b_ple_gate_2"], None, part=1)
            wpg = a["w_ple_gate_2"].rearrange("a k n -> (a k) n")
            for j in range(4):
                load(f"pg{j}", rows(wpg, 2 * j), "p (k n) -> p k n", k=2)

        @block.tensor
        def _(pe):
            for s in range(RING):
                pe.sem_inc(used[s].sem, 1)
            for b in range(8):
                pe.sem_inc(emptied[b].sem, 1)

            def open_bank(b, name):
                emptied[b].add(name)
                pe.wait_ge(emptied[b].sem, emptied[b].at(name))

            def arrived(name, plus=0):
                s = slot_of[name]
                pe.wait_ge(loaded[s].sem, loaded[s].at(name, plus))
                return s

            def by_columns(name, bank, x, key_=None):
                open_bank(bank, name)
                s = arrived(name)
                for pt in range(2):
                    for k in range(DT):
                        mm = pe.matmul(ps[:, bank, pt * T:pt * T + T],
                                       ring[:, s, k * CH + pt * P:k * CH + pt * P + P], x[:, k, :],
                                       start=(k == 0), stop=(k == DT - 1))
                mm.then_inc(used[s].sem, 1)

            def by_rows(name, lhs, is_first, is_last, plus=0):
                s = arrived(name, plus)
                for kk in range(2):
                    for t in range(TT):
                        for half in range(2):
                            mm = pe.matmul(ps[:, 4 + 2 * t + half, :], lhs(kk, t),
                                           ring[:, s, kk * D + half * 512:kk * D + half * 512 + 512],
                                           start=(is_first and kk == 0), stop=(is_last and kk == 1))
                mm.then_inc(used[s].sem, 1)

            def open_acc(name):
                for b in range(4, 8):
                    open_bank(b, name)

            def transposes(tag, src, ready):
                for t in range(TT):
                    ready(t)
                    for j in range(4):
                        if t == 0:
                            open_bank(j, ("T", tag))
                        for kk in range(2):
                            k = 2 * j + kk
                            mm = pe.transpose(ps[:, j, kk * T + t * P:kk * T + t * P + P],
                                              src[:, t, k * P:k * P + P], ident[:])
                mm.then_inc(pe_full.add(("T", tag)), 1)
                for j in range(4):
                    pe.wait_ge(emptied[j].sem, emptied[j].at(("T", tag), 1))

            def after_ln(tag):
                def ready(t):
                    pe.wait_ge(dve_done.sem, dve_done.at(("hn", tag, t)))
                transposes(tag, hn, ready)

            def ffn(tag):
                def gate_up(c):
                    by_columns(key(tag, "gate", c), 2 * (c % 2), hT)
                    by_columns(key(tag, "up", c), 2 * (c % 2) + 1, hT)

                def down(c, i=None):
                    b = 2 * (c % 2) + 1
                    pe.wait_ge(emptied[b].sem, emptied[b].at(key(tag, "up", c), 1 if i is None else i * 2 + 1))
                    hid = w(FK + 512 * (c % 2) + 0, 512)
                    by_rows(key(tag, "down", c), lambda kk, t: hid[:, kk * T + t * P:kk * T + t * P + P],
                            c == 0, c == NCH - 1, 0 if i is None else i)

                gate_up(0)
                gate_up(1)
                open_acc((tag, "acc"))
                down(0)
                with counted(book, pe, "c" + tag, 2, emptied + [pe_full]) as i:
                    gate_up(2)
                    down(1, i)
                    for c in range(3, 6):
                        gate_up(c)
                        down(c - 1)
                gate_up(10)
                down_last(tag)
                down(10)

            def down_last(tag):
                c = 5
                pe.wait_ge(emptied[3].sem, emptied[3].at(key(tag, "up", c), 1, **{"c" + tag: 1}))
                hid = w(FK + 512, 512)
                s = slot_of[key(tag, "down", c)]
                pe.wait_ge(loaded[s].sem, loaded[s].at(key(tag, "down", c), **{"c" + tag: 1}))
                for kk in range(2):
                    for t in range(TT):
                        for half in range(2):
                            mm = pe.matmul(ps[:, 4 + 2 * t + half, :], hid[:, kk * T + t * P:kk * T + t * P + P],
                                           ring[:, s, kk * D + half * 512:kk * D + half * 512 + 512],
                                           start=False, stop=False)
                mm.then_inc(used[s].sem, 1)

            def level(tag, lv):
                if lv == 0:
                    kk, qq = w(K, 1024), w(Q, 1024)
                else:
                    kk, qq = fk, fq
                    pe.wait_ge(dve_done.sem, dve_done.at(("F", tag, lv)))
                if lv == 8:
                    open_bank(6, ("A", tag, lv, 0))
                    for hd in range(HEADS):
                        mm = pe.matmul(ps[:, 6, hd * P:hd * P + P], kk[:, hd * T:hd * T + P],
                                       qq[:, hd * T + P:hd * T + T], start=True, stop=True)
                    mm.then_inc(pe_full.add(("A", tag, lv, 0)), 1)
                    return
                for t in range(TT):
                    b = (6 if lv % 2 == 0 else 2) + t
                    open_bank(b, ("A", tag, lv, t))
                    for hd in range(HEADS):
                        o = hd * T + t * P
                        mm = pe.matmul(ps[:, b, hd * P:hd * P + P], kk[:, o:o + P], qq[:, o:o + P],
                                       start=True, stop=True)
                    mm.then_inc(pe_full.add(("A", tag, lv, t)), 1)

            def outputs(tag, units, vals):
                per = units // HEADS
                pe.wait_ge(dve_done.sem, dve_done.at(("attn", tag)))
                for j in range(units // 2):
                    b = obank(tag, j)
                    open_bank(b, ("O", tag, j))
                    for uu in range(2):
                        u = 2 * j + uu
                        hd = u // per
                        pe.matmul(ps[:, b, uu * T:uu * T + P], vals[:, 0, u * P:u * P + P],
                                  attn[:, 0, hd, :], start=True, stop=True)
                        pe.matmul(ps[:, b, uu * T + P:uu * T + T], vals[:, 0, u * P:u * P + P],
                                  cross[:, hd, :], start=True, stop=False)
                        mm = pe.matmul(ps[:, b, uu * T + P:uu * T + T], vals[:, 1, u * P:u * P + P],
                                       attn[:, 1, hd, :], start=False, stop=True)
                    mm.then_inc(pe_full.add(("O", tag, j)), 1)

            pe.wait_ge(first.sem, 16 * 6)
            pe.wait_ge(prm.sem, prm.at("rows"))
            open_bank(0, "params")
            for b, n in enumerate((128, 102, 32)):
                mm = pe.transpose(ps[:, 0, b * P:b * P + n], work[0:n, Y + b * P:Y + b * P + P], ident[0:n, 0:n])
            mm.then_inc(pe_full.add("params"), 1)
            transposes("x", h, lambda t: None)
            transposes("mem", w(KT, 2048, "p (t n) -> p t n", t=TT), lambda t: None)
            pe.wait_ge(dve_done.sem, dve_done.at("consts"))

            with counted(book, pe, "L", LAYERS, emptied + [pe_full]) as L:
                ffn("f1")
                after_ln(0)
                by_columns("rf0", 0, hT)
                by_columns("rf1", 1, hT)
                by_columns("rq0", 2, hT)
                by_columns("rq1", 3, hT)
                by_columns("cc", 0, hT)
                pe.wait_ge(emptied[2].sem, emptied[2].at("rq0", 1))
                pe.wait_ge(emptied[3].sem, emptied[3].at("rq1", 1))
                pe.wait_ge(dve_done.sem, dve_done.at(("k", "r")))
                level("r", 0)
                by_columns("ch", 1, hT)
                level("r", 1)
                by_columns("cb", 0, hT)
                level("r", 2)
                by_columns("pu", 1, hT)
                level("r", 3)
                for t in range(TT):
                    open_bank(4 + t, "ri")
                for j in range(2):
                    s = arrived(f"ri{j}")
                    for t in range(TT):
                        for k in range(4):
                            mm = pe.matmul(ps[:, 4 + t, :], hT[:, 4 * j + k, t * P:t * P + P],
                                           ring[:, s, k * 512:k * 512 + 512],
                                           start=(j == 0 and k == 0), stop=(j == 1 and k == 3))
                    mm.then_inc(used[s].sem, 1)
                level("r", 4)
                for j in range(4):
                    by_columns(f"ck{j}", j % 2, memT)
                    level("r", 5 + j)
                open_bank(2, "pool")
                pe.wait_ge(pool_done.sem, pool_done.at("pooled"))
                pe.wait_ge(prm.sem, prm.at(("wpool", 3)))
                pm = w(PM, 512)
                for kt in range(2):
                    mm = pe.matmul(ps[:, 2, kt * T:kt * T + T], wpool[:, kt, :], pm[:, kt * T:kt * T + T],
                                   start=True, stop=True)
                mm.then_inc(pe_full.add("pool"), 1)
                open_acc("cv")
                for j in range(4):
                    by_rows(f"cv{j}", lambda kk, t: memT[:, 2 * j + kk, t * P:t * P + P], j == 0, j == 3)
                for t in range(TT):
                    pe.wait_ge(emptied[4 + t].sem, emptied[4 + t].at("ri", 1))
                outputs("r", 4, w(V, 1024, "p (t n) -> p t n", t=TT))
                by_columns("rg0", 0, hT)
                by_columns("rg1", 1, hT)
                for j in range(2):
                    open_bank(j, ("ms", "r", j))
                    pe.wait_ge(act_done.sem, act_done.at(("sq", "r", j)))
                    pe.matmul(ps[:, j, :], ones[:], work[:, PR + 512 * j:PR + 512 * j + 512], start=True, stop=True)\
                        .then_inc(pe_full.add(("ms", "r", j)), 1)
                open_acc("wo")
                for j, k0 in enumerate((0, 6, 2, 4)):
                    if j == 0:
                        pe.wait_ge(pool_done.sem, pool_done.at("conv"))
                    if j == 1:
                        pe.wait_ge(emptied[2].sem, emptied[2].at("pool", 1))
                    if j >= 2:
                        pe.wait_ge(dve_done.sem, dve_done.at(("y", "r", j - 2)))
                    by_rows(f"wo{j}", lambda kk, t: yT[:, k0 + kk, t * P:t * P + P], j == 0, j == 3)
                after_ln(1)

                def scores(hd):
                    pe.wait_ge(emptied[2 + hd % 2].sem, emptied[2 + hd % 2].at(f"cq{hd}", 1))
                    b = hd % 2
                    open_bank(b, ("sc", hd))
                    for t in range(TT):
                        for kk in range(2):
                            mm = pe.matmul(ps[:, b, t * T:t * T + T],
                                           work[:, Q + (2 * hd + kk) * T + t * P:Q + (2 * hd + kk) * T + t * P + P],
                                           keyT[:, 2 * hd + kk, :], start=(kk == 0), stop=(kk == 1))
                    mm.then_inc(pe_full.add(("sc", hd)), 1)

                def weighted(hd):
                    pe.wait_ge(dve_done.sem, dve_done.at(("p", hd)))
                    open_bank(2, ("pT", hd))
                    prob = w(FQ + 512 * (hd % 2), 512, "p (t m) -> p t m", t=TT)
                    for t in range(TT):
                        for mt in range(2):
                            mm = pe.transpose(ps[:, 2, mt * T + t * P:mt * T + t * P + P],
                                              prob[:, t, mt * P:mt * P + P], ident[:])
                    mm.then_inc(pe_full.add(("pT", hd)), 1)
                    pe.wait_ge(emptied[2].sem, emptied[2].at(("pT", hd), 1))
                    open_bank(3, ("co", hd))
                    pT = w(FK + 512 * (hd % 2), 512, "p (m t) -> p m t", m=2)
                    for dd in range(2):
                        for mt in range(2):
                            c0 = hd * 256 + dd * P
                            mm = pe.matmul(ps[:, 3, dd * T:dd * T + T], valm[:, mt, c0:c0 + P], pT[:, mt, :],
                                           start=(mt == 0), stop=(mt == 1))
                    mm.then_inc(pe_full.add(("co", hd)), 1)

                by_columns("cq0", 2, hT)
                by_columns("cq1", 3, hT)
                scores(0)
                by_columns("cq2", 2, hT)
                scores(1)
                by_columns("cq3", 3, hT)
                weighted(0)
                scores(2)
                weighted(1)
                scores(3)
                weighted(2)
                weighted(3)
                open_acc("co")
                for j in range(4):
                    pe.wait_ge(emptied[3].sem, emptied[3].at(("co", j), 1))
                    by_rows(f"co{j}", lambda kk, t: w(PR, 2048, "p (g t) -> p g t", g=8)[:, 2 * j + kk, t * P:t * P + P],
                            j == 0, j == 3)
                after_ln(2)
                ffn("f2")
                after_ln(3)

            for j in range(4):
                by_columns(f"xa{j}", j, hT)
            for j in range(2):
                by_columns(f"q{j}", j, hT)
            for j in range(2):
                by_columns(f"k{j}", 2 + j, hT)
            open_bank(0, "glr")
            s = arrived("glr")
            for k in range(DT):
                mm = pe.matmul(ps[0:16, 0, 0:T], ring[:, s, k * 16:k * 16 + 16], hT[:, k, :],
                               start=(k == 0), stop=(k == DT - 1))
            mm.then_inc(used[s].sem, 1)
            open_acc("v")
            for j in range(4):
                by_rows(f"v{j}", lambda kk, t: hT[:, 2 * j + kk, t * P:t * P + P], j == 0, j == 3)
            pe.wait_ge(emptied[0].sem, emptied[0].at("glr", 1))
            s = arrived("glg")
            for j in range(2):
                open_bank(j, ("zg", j))
                for kk in range(2):
                    c0 = (2 * j + kk) * P
                    mm = pe.matmul(ps[:, j, kk * T:kk * T + T], ring[0:16, s, c0:c0 + P], work[0:16, FQ:FQ + T],
                                   start=True, stop=True)
                if j == 0:
                    mm.then_inc(pe_full.add(("zg", 0)), 1)
            mm.then_inc(used[s].sem, 1)
            pe.wait_ge(dve_done.sem, dve_done.at("xc"))
            for which in ("r", "i"):
                s = arrived("lru" + which)
                for j in range(4):
                    b = 2 + j % 2
                    open_bank(b, ("lru", which, j))
                    for kk in range(2):
                        g = 2 * j + kk
                        mm = pe.matmul(ps[:, b, kk * T:kk * T + T], ring[:, s, g * P:g * P + P],
                                       work[:, XC + g * T:XC + g * T + T], start=True, stop=True)
                    if j < 3:
                        mm.then_inc(pe_full.add(("lru", which, j)), 1)
                mm.then_inc(used[s].sem, 1)
            for j in range(4):
                by_columns(f"go{j}", j % 2, hT)
            for j in range(2):
                pe.wait_ge(emptied[j].sem, emptied[j].at(f"q{j}", 1))
                pe.wait_ge(emptied[2 + j].sem, emptied[2 + j].at(f"k{j}", 1))
            level("g", 0)
            for j in range(4):
                by_columns(f"mb{j}", j % 2, hT)
                level("g", 1 + j)
            for j in range(4):
                by_columns(f"ga{j}", j % 2, hT)
                level("g", 5 + j)
            for b in range(4, 8):
                pe.wait_ge(emptied[b].sem, emptied[b].at("v", 1))
            outputs("g", 8, w(V, 2048, "p (t n) -> p t n", t=TT))
            for j in range(4):
                by_columns(f"ma{j}", j % 2, hT)
            for j in range(2):
                open_bank(j, ("ms", "g", j))
                for hh in range(2):
                    pe.wait_ge(act_done.sem, act_done.at(("sq", "g", 2 * j + hh)))
                    for uu in range(2):
                        u = 2 * (2 * j + hh) + uu
                        mm = pe.matmul(ps[:, j, hh * T:hh * T + T], ones[:], work[:, PR + u * T:PR + u * T + T],
                                       start=(uu == 0), stop=(uu == 1))
                mm.then_inc(pe_full.add(("ms", "g", j)), 1)
            open_acc("w2o")
            for j in range(4):
                pe.wait_ge(dve_done.sem, dve_done.at(("y", "g", j)))
                by_rows(f"w2o{j}", lambda kk, t: yT[:, 2 * j + kk, t * P:t * P + P], j == 0, j == 3)
            after_ln("A")

            open_bank(0, "router")
            s = arrived("router")
            for t in range(TT):
                pe.matmul(ps[:, 0, t * 32:t * 32 + 32], ones[0:1, :], brout[0:1, :], start=True, stop=False)
                for k in range(DT):
                    mm = pe.matmul(ps[:, 0, t * 32:t * 32 + 32], hT[:, k, t * P:t * P + P],
                                   ring[:, s, k * 32:k * 32 + 32], start=False, stop=(k == DT - 1))
            mm.then_inc(used[s].sem, 1)
            open_bank(1, "bup")
            s = arrived("bup")
            for b in range(4):
                mm = pe.transpose(ps[:, 1, b * P:b * P + P], ring[:, s, b * P:b * P + P], ident[:])
            mm.then_inc(used[s].sem, 1)
            open_bank(2, "gT")
            pe.wait_ge(dve_done.sem, dve_done.at("gates"))
            for t in range(TT):
                mm = pe.transpose(ps[0:32, 2, t * P:t * P + P], work[:, GATES + t * 32:GATES + t * 32 + 32], ident[:])
            mm.then_inc(pe_full.add("gT"), 1)
            pe.wait_ge(emptied[2].sem, emptied[2].at("gT", 1))
            open_acc("bd")
            s = arrived("bdown")
            for t in range(TT):
                for half in range(2):
                    mm = pe.matmul(ps[:, 4 + 2 * t + half, :], work[0:32, GT + t * P:GT + t * P + P],
                                   ring[0:32, s, half * 512:half * 512 + 512], start=True, stop=True)
            mm.then_inc(used[s].sem, 1)

            with counted(book, pe, "e", EXPERTS, emptied + [pe_full]) as e:
                def gate_up(j):
                    by_columns(("moe", "g", j), 2 * (j % 2), hT)
                    by_columns(("moe", "u", j), 2 * (j % 2) + 1, hT)

                def down(j):
                    pe.wait_ge(dve_done.sem, dve_done.at(("act", j)))
                    by_rows(("moe", "d", j), lambda kk, t: work[:, ACTT + (2 * j + kk) * T + t * P:ACTT + (2 * j + kk) * T + t * P + P],
                            j == 0, j == 3)

                gate_up(0)
                gate_up(1)
                open_acc("moe")
                down(0)
                gate_up(2)
                down(1)
                gate_up(3)
                down(2)
                down(3)

            open_bank(0, "ptok")
            s = arrived("ptok")
            for t in range(TT):
                for kt in range(2):
                    mm = pe.transpose(ps[:, 0, kt * T + t * P:kt * T + t * P + P],
                                      ring[:, s, t * 256 + kt * P:t * 256 + kt * P + P], ident[:])
            mm.then_inc(used[s].sem, 1)
            pe.wait_ge(emptied[0].sem, emptied[0].at("ptok", 1))
            after_ln("B")
            s = arrived("bpg")
            open_acc("pg")
            for t in range(TT):
                for half in range(2):
                    mm = pe.matmul(ps[:, 4 + 2 * t + half, :], ones[0:1, :], ring[0:1, s, half * 512:half * 512 + 512],
                                   start=True, stop=False)
            mm.then_inc(used[s].sem, 1)
            for j in range(4):
                by_rows(f"pg{j}", lambda kk, t: hT[:, 2 * j + kk, t * P:t * P + P], False, j == 3)
            s = arrived("wple")
            for t in range(TT):
                for half in range(2):
                    b = 2 * t + half
                    open_bank(b, "ple")
                    for kk in range(2):
                        mm = pe.matmul(ps[:, b, :], work[:, FQ + kk * T + t * P:FQ + kk * T + t * P + P],
                                       ring[:, s, kk * D + half * 512:kk * D + half * 512 + 512],
                                       start=(kk == 0), stop=(kk == 1))
            mm.then_inc(used[s].sem, 1)

        @block.scalar
        def _(act):
            def done(ins, name):
                ins.then_inc(act_done.add(name), 1)

            def mine(name):
                act.wait_ge(act_done.sem, act_done.at(name))

            def copy_out(name, bank, dst, full):
                full()
                nc.scalar.copy(dst, ps[:, bank, :]).then_inc(emptied[bank].sem, 1)

            def pe_group(name):
                act.wait_ge(pe_full.sem, pe_full.at(name))

            def row(name, b, at):
                src = a[name]
                flat = {1: "a -> a", 2: "a n -> (a n)", 3: "a b n -> (a b n)"}[len(src.shape)]
                v = src.rearrange(flat).rearrange("(r n) -> r n", n=P)
                act.dma_start(work[at:at + v.shape[0], Y + b * P:Y + b * P + P], v)\
                    .then_inc(prm.add("rows" if name == "ln2_b_2" else ("row", name)), 16)

            for b, group in enumerate((COLS1, COLS2, COLS3)):
                at = 0
                for nm, n in group:
                    row(nm, b, at)
                    at += n

            def evac_T(tag, gname=None, i=None, dst=None):
                pe_group(("T", tag))
                for k in range(4):
                    bank = ps[:, k // 2, (k % 2) * T:(k % 2) * T + T]
                    if gname is None:
                        ins = nc.scalar.copy(dst[:, k, :], bank)
                    else:
                        ins = nc.scalar.activation(dst[:, k, :], bank, ACT.Identity,
                                                   bias=col(gname[1], i + k), scale=col(gname[0], i + k))
                    if k % 2:
                        ins.then_inc(emptied[k // 2].sem, 1)

            def ln(tag, gname, i):
                act.wait_ge(dve_done.sem, dve_done.at(("var", tag)))
                done(nc.scalar.activation(rstd[:], mv[:, :, 1], ACT.Sqrt, bias=epsc[:, 0:1]), ("std", tag))
                evac_T(tag, gname, i, hT)

            def ffn(tag):
                def gate(c):
                    slot_used(act, key(tag, "gate", c))
                    nc.scalar.activation(w(FQ + 512 * (c % 2), 512), ps[:, 2 * (c % 2), :], ACT.Silu)\
                        .then_inc(emptied[2 * (c % 2)].sem, 1)
                gate(0)
                gate(1)
                with counted(book, act, "c" + tag, 2, [act_done]):
                    for c in range(2, 6):
                        gate(c)
                gate(10)

            def squares(tag, units):
                for j in range(units // 2):
                    pe_group(("O", tag, j))
                    done(nc.scalar.activation(work[:, PR + 512 * j:PR + 512 * j + 512], ps[:, obank(tag, j), :],
                                              ACT.Square), ("sq", tag, j))

            def roots(tag, n, eps):
                for j in range(2):
                    pe_group(("ms", tag, j))
                    nc.scalar.activation(work[:, Q + 512 * j:Q + 512 * j + 512], ps[:, j, :], ACT.Sqrt,
                                         bias=epsc[:, eps:eps + 1], scale=1.0 / n).then_inc(emptied[j].sem, 1)

            pe_group("params")
            flat = cols[:].rearrange("p b n -> p (b n)")
            nc.scalar.copy(flat[:, 0:230], ps[:, 0, 0:230])
            nc.scalar.copy(flat[:, 256:288], ps[:, 0, 256:288]).then_inc(emptied[0].sem, 1)
            act.wait_ge(emptied[0].sem, emptied[0].at("params", 1))
            evac_T("x", dst=hT)
            evac_T("mem", dst=memT)
            done(nc.scalar.activation(small[:, 0:8], col("lru_lambda_2", 0, 8), ACT.Abs), "abs")
            mine("abs")
            done(nc.scalar.activation(small[:, 8:16], small[:, 0:8], ACT.Exp, scale=-1.0), "lexp")
            mine("lexp")
            act.wait_ge(dve_done.sem, dve_done.at("consts0"))
            done(nc.scalar.activation(small[:, 16:24], small[:, 8:16], ACT.Ln, bias=epsc[:, 2:3]), "lln")
            done(nc.scalar.activation(small[:, 32:40], small[:, 24:32], ACT.Exp), "lbexp")

            with counted(book, act, "L", LAYERS, [act_done, prm]) as L:
                for g in range(4):
                    lo = 64 * (g % 2)
                    act.dma_start(wpool[lo:lo + 64, g // 2, lo:lo + 64],
                                  a["pool_w"].rearrange("l g c d -> c (l g) d")[:, bass.ds(L * 4 + g, 1), :]
                                  .rearrange("c a d -> c (a d)")).then_inc(prm.add(("wpool", g)), 16)
                ffn("f1")
                ln(0, ("ln_g", "ln_b"), L * 32)
                for j in range(2):
                    slot_used(act, f"rf{j}")
                    nc.scalar.activation(work[:, FQ + 512 * j:FQ + 512 * j + 512], ps[:, j, :], ACT.Sigmoid)\
                        .then_inc(emptied[j].sem, 1)
                for j in range(2):
                    copy_out(None, 2 + j, work[:, Q + 512 * j:Q + 512 * j + 512], lambda: slot_used(act, f"rq{j}"))
                copy_out(None, 0, w(CC, 512), lambda: slot_used(act, "cc"))
                slot_used(act, "cb")
                act.wait_ge(emptied[1].sem, emptied[1].at("ch", 1))
                nc.scalar.copy(w(CC, 512), ps[:, 0, :]).then_inc(emptied[0].sem, 1)
                slot_used(act, "pu")
                nc.scalar.copy(w(PU, 544, "p (g t) -> p g t", g=2)[:, :, 16:272],
                               ps[:, 1, :].rearrange("p (g t) -> p g t", g=2)).then_inc(emptied[1].sem, 1)
                slot_used(act, "ri1")
                for t in range(TT):
                    nc.scalar.copy(work[:, V + 512 * t:V + 512 * t + 512], ps[:, 4 + t, :])\
                        .then_inc(emptied[4 + t].sem, 1)
                for j in range(4):
                    copy_out(None, j % 2, work[:, KT + 512 * j:KT + 512 * j + 512], lambda: slot_used(act, f"ck{j}"))
                pe_group("pool")
                for kt in range(2):
                    ins = nc.scalar.mul(yT[:, 6 + kt, :], ps[:, 2, kt * T:kt * T + T], col("pool_scale", L * 2 + kt))
                ins.then_inc(emptied[2].sem, 1)
                slot_used(act, "cv3")
                for b in range(4, 8):
                    t, half = (b - 4) // 2, b % 2
                    nc.scalar.copy(valm[:, t, half * 512:half * 512 + 512], ps[:, b, :]).then_inc(emptied[b].sem, 1)
                squares("r", 4)
                for j in range(2):
                    slot_used(act, f"rg{j}")
                    nc.scalar.activation(work[:, Y + 512 + 512 * j:Y + 1024 + 512 * j], ps[:, j, :], ACT.Sigmoid)\
                        .then_inc(emptied[j].sem, 1)
                roots("r", 128, 1)
                ln(1, ("ln_g", "ln_b"), L * 32 + 8)

                def q_copy(j):
                    copy_out(None, 2 + j % 2, work[:, Q + 512 * j:Q + 512 * j + 512], lambda: slot_used(act, f"cq{j}"))

                def expo(hd):
                    b = hd % 2
                    act.wait_ge(dve_done.sem, dve_done.at(("nm", hd)))
                    for t in range(TT):
                        ins = nc.scalar.activation(work[:, FQ + 512 * b + t * T:FQ + 512 * b + t * T + T],
                                                   ps[:, b, t * T:t * T + T], ACT.Exp, bias=smax[:, hd, t:t + 1],
                                                   scale=1.0 / 16, accum_out=ssum[:, hd, t:t + 1])
                        if t == 1:
                            ins.then_inc(emptied[b].sem, 1)

                def p_copy(hd):
                    copy_out(None, 2, w(FK + 512 * (hd % 2), 512), lambda: pe_group(("pT", hd)))

                q_copy(0)
                q_copy(1)
                expo(0)
                q_copy(2)
                expo(1)
                q_copy(3)
                p_copy(0)
                expo(2)
                p_copy(1)
                expo(3)
                p_copy(2)
                p_copy(3)
                ln(2, ("ln_g", "ln_b"), L * 32 + 16)
                ffn("f2")
                ln(3, ("ln_g", "ln_b"), L * 32 + 24)

            xa = w(XA, 2072, "p (g t) -> p g t", g=8)
            for j in range(4):
                slot_used(act, f"xa{j}")
                nc.scalar.copy(xa[:, 2 * j:2 * j + 2, 3:259], ps[:, j, :].rearrange("p (g t) -> p g t", g=2))\
                    .then_inc(emptied[j].sem, 1)
            for j in range(2):
                slot_used(act, f"q{j}")
                nc.scalar.mul(work[:, Q + 512 * j:Q + 512 * j + 512], ps[:, j, :], float(P) ** -0.5)\
                    .then_inc(emptied[j].sem, 1)
            for j in range(2):
                copy_out(None, 2 + j, work[:, K + 512 * j:K + 512 * j + 512], lambda: slot_used(act, f"k{j}"))
            slot_used(act, "glr")
            nc.scalar.copy(work[0:16, FQ:FQ + T], ps[0:16, 0, 0:T]).then_inc(emptied[0].sem, 1)
            slot_used(act, "v3")
            for b in range(4, 8):
                t, half = (b - 4) // 2, b % 2
                nc.scalar.copy(work[:, V + t * D + half * 512:V + t * D + half * 512 + 512], ps[:, b, :])\
                    .then_inc(emptied[b].sem, 1)
            for hd in range(HEADS):
                if hd == 0:
                    pe_group(("zg", 0))
                if hd == 2:
                    slot_used(act, "glg")
                ins = nc.scalar.activation(pr[:, hd, :], ps[:, hd // 2, (hd % 2) * T:(hd % 2) * T + T], ACT.Abs,
                                           bias=col("gla_b_gate_2", hd))
                done(ins, ("zabs", hd))
            mine(("zabs", 3))
            done(nc.scalar.activation(w(PR, 1024), w(PR, 1024), ACT.Exp, scale=-1.0), "zexp")
            mine("zexp")
            done(nc.scalar.activation(w(PR, 1024), w(PR, 1024), ACT.Ln, bias=epsc[:, 2:3]), "zln")
            act.wait_ge(dve_done.sem, dve_done.at("logsig"))
            done(nc.scalar.activation(w(PR, 1024), w(SU, 1024), ACT.Exp, scale=1.0 / 16), "decay")
            for which, off, bias in (("r", R, "lru_b_r_2"), ("i", IG, "lru_b_i_2")):
                for j in range(4):
                    b = 2 + j % 2
                    if j < 3:
                        pe_group(("lru", which, j))
                    else:
                        slot_used(act, "lru" + which)
                    for kk in range(2):
                        g = 2 * j + kk
                        ins = nc.scalar.activation(work[:, off + g * T:off + g * T + T], ps[:, b, kk * T:kk * T + T],
                                                   ACT.Sigmoid, bias=col(bias, g))
                    ins.then_inc(emptied[b].sem, 1)
            act.wait_ge(emptied[3].sem, emptied[3].at(("lru", "i", 3), 1))
            for g in range(8):
                ins = nc.scalar.activation(work[:, TH + g * T:TH + g * T + T], work[:, R + g * T:R + g * T + T],
                                           ACT.Tanh, scale=sp8[:, 0, g:g + 1])
            done(ins, "tanh")
            mine("tanh")
            for g in range(8):
                ins = nc.scalar.activation(work[:, R + g * T:R + g * T + T], work[:, R + g * T:R + g * T + T],
                                           ACT.Exp, scale=sp8[:, 1, g:g + 1])
            done(ins, "a")
            act.wait_ge(dve_done.sem, dve_done.at("ratio"))
            done(nc.scalar.activation(w(TH, 2048), w(TH, 2048), ACT.Sqrt, scale=2.0), "mult")
            act.wait_ge(h_ready.sem, h_ready.at(("h", 3), L=LAYERS - 1))
            gob = hn[:].rearrange("p t n -> p (t n)")
            for j in range(4):
                slot_used(act, f"go{j}")
                nc.scalar.activation(gob[:, 512 * j:512 * j + 512], ps[:, j % 2, :], ACT.Silu)\
                    .then_inc(emptied[j % 2].sem, 1)
            for j in range(4):
                slot_used(act, f"mb{j}")
                if j >= 2:
                    act.wait_ge(pool_done.sem, pool_done.at(("mb", j - 2)))
                if j == 0:
                    act.wait_ge(dve_done.sem, dve_done.at("scan"))
                nc.scalar.activation(work[:, TH + 512 * (j % 2):TH + 512 * (j % 2) + 512], ps[:, j % 2, :],
                                     ACT.Sigmoid).then_inc(emptied[j % 2].sem, 1)
            for nm, fn in (("ga", ACT.Gelu_apprx_tanh), ("ma", ACT.Sigmoid)):
                if nm == "ma":
                    squares("g", 8)
                for j in range(4):
                    slot_used(act, f"{nm}{j}")
                    if j >= 2:
                        act.wait_ge(dve_done.sem, dve_done.at((nm, j - 2)))
                    elif nm == "ma":
                        act.wait_ge(dve_done.sem, dve_done.at(("ga", 2 + j)))
                    nc.scalar.activation(work[:, R + 512 * (j % 2):R + 512 * (j % 2) + 512], ps[:, j % 2, :], fn)\
                        .then_inc(emptied[j % 2].sem, 1)
            roots("g", 256, 0)
            ln("A", ("ln1_g_2", "ln1_b_2"), 0)

            act.wait_ge(dve_done.sem, dve_done.at("rmax"))
            for t in range(TT):
                ins = nc.scalar.activation(work[:, GATES + t * 32:GATES + t * 32 + 32],
                                           work[:, LOGIT + t * 32:LOGIT + t * 32 + 32], ACT.Exp,
                                           bias=small[:, 40 + t:41 + t])
            done(ins, "rexp")
            slot_used(act, "bup")
            nc.scalar.copy(w(BUP, 512), ps[:, 1, :]).then_inc(emptied[1].sem, 1)
            pe_group("gT")
            nc.scalar.copy(work[0:32, GT:GT + T], ps[0:32, 2, 0:T]).then_inc(emptied[2].sem, 1)
            with counted(book, act, "e", EXPERTS, [act_done]) as e:
                for j in range(4):
                    act.wait_ge(emptied[2 * (j % 2)].sem, emptied[2 * (j % 2)].at(("moe", "g", j), 1))
                    done(nc.scalar.activation(work[:, SG + 512 * (j % 2):SG + 512 * (j % 2) + 512],
                                              work[:, GH + 512 * (j % 2):GH + 512 * (j % 2) + 512],
                                              ACT.Sigmoid, scale=SIG_ALPHA), ("sg", j))
            slot_used(act, "ptok")
            nc.scalar.copy(w(FQ, 512), ps[:, 0, :]).then_inc(emptied[0].sem, 1)
            ln("B", ("ln2_g_2", "ln2_b_2"), 0)
            slot_used(act, "pg3")
            act.wait_ge(h_ready.sem, h_ready.at(("h", "B")))
            for b in range(4, 8):
                t, half = (b - 4) // 2, b % 2
                nc.scalar.activation(hn[:, t, half * 512:half * 512 + 512], ps[:, b, :], ACT.Sigmoid)\
                    .then_inc(emptied[b].sem, 1)
            for t in range(TT):
                act.wait_ge(dve_done.sem, dve_done.at(("out", t)))
                act.dma_start(a["out"].rearrange("a (t p) n -> p (a t) n", p=P)[:, t, :], h[:, t, :])\
                    .then_inc(out_done.add(t), 16)
            act.wait_ge(out_done.sem, 32)

        @block.vector
        def _(dve):
            v = nc.vector

            def done(ins, name):
                ins.then_inc(dve_done.add(name), 1)

            def link(ins):
                name = ("link", dve_done.n, tuple(dve_done.loops))
                ins.then_inc(dve_done.add(name), 1)
                dve.wait_ge(dve_done.sem, dve_done.at(name))

            def mine(name):
                dve.wait_ge(dve_done.sem, dve_done.at(name))

            def pe_group(name):
                dve.wait_ge(pe_full.sem, pe_full.at(name))

            def bank_empty(b, name, **iters):
                dve.wait_ge(emptied[b].sem, emptied[b].at(name, 1, **iters))

            def evac_T(tag, gname=None, i=None, dst=None):
                pe_group(("T", tag))
                for k in range(4, 8):
                    bank = ps[:, k // 2, (k % 2) * T:(k % 2) * T + T]
                    if gname is None:
                        ins = v.tensor_copy(dst[:, k, :], bank)
                    else:
                        ins = v.tensor_scalar(dst[:, k, :], bank, col(gname[0], i + k), col(gname[1], i + k),
                                              ALU.mult, ALU.add)
                    if k % 2:
                        ins.then_inc(emptied[k // 2].sem, 1)

            def ln(tag, gname, i, alpha, full, banked=True):
                full()
                dve.wait_ge(h_ready.sem, h_ready.at(("h", tag), -1))
                for t in range(TT):
                    for half in range(2):
                        c = slice(half * 512, half * 512 + 512)
                        src = ps[:, 4 + 2 * t + half, :] if banked else \
                            work[:, MACC + t * D + half * 512:MACC + t * D + half * 512 + 512]
                        ins = v.scalar_tensor_tensor(out=hn[:, t, c], in0=h[:, t, c], scalar=alpha, in1=src,
                                                     op0=ALU.mult, op1=ALU.add)
                        if banked:
                            ins.then_inc(emptied[4 + 2 * t + half].sem, 1)
                        else:
                            done(ins, ("x", tag, t, half))
                for t in range(TT):
                    for half in range(2):
                        if banked:
                            bank_empty(4 + 2 * t + half, acc_name(tag))
                        else:
                            mine(("x", tag, t, half))
                        ins = v.bn_stats(stat[:, t, half, :], hn[:, t, half * 512:half * 512 + 512])
                    done(ins, ("stats", tag, t))
                for t in range(TT):
                    mine(("stats", tag, t))
                    plain(dve)
                    ins = v.bn_aggr(mv[:, t, :], stat[:, t, :, :].rearrange("p a b -> p (a b)"))
                done(ins, ("var", tag))
                dve.wait_ge(act_done.sem, act_done.at(("std", tag)))
                link(v.reciprocal(rstd[:], rstd[:]))
                for t in range(TT):
                    done(v.tensor_scalar(hn[:, t, :], hn[:, t, :], mv[:, t, 0:1], rstd[:, t:t + 1],
                                         ALU.subtract, ALU.mult), ("hn", tag, t))
                evac_T(tag, gname, i, hT)

            def acc_name(tag):
                return {0: ("f1", "acc"), 1: "wo", 2: "co", 3: ("f2", "acc"), "A": "w2o"}[tag]

            def ffn(tag):
                def up(c):
                    b = 2 * (c % 2) + 1
                    slot_used(dve, key(tag, "up", c))
                    bank_empty(b - 1, key(tag, "gate", c))
                    v.scalar_tensor_tensor(out=w(FK + 512 * (c % 2), 512), in0=w(FQ + 512 * (c % 2), 512), scalar=0.5,
                                           in1=ps[:, b, :], op0=ALU.mult, op1=ALU.mult).then_inc(emptied[b].sem, 1)
                up(0)
                up(1)
                with counted(book, dve, "c" + tag, 2, [dve_done]):
                    for c in range(2, 6):
                        up(c)
                up(10)

            def decay_step(tag, lv):
                n = 1 << (lv - 1)

                def halves(off):
                    x = w(off, 1024, "p (b a n) -> p b a n", a=2, n=n)
                    return x[:, :, 0, :], x[:, :, 1, :]

                nb = 1024 // (2 * n)
                (q0, q1), (k0, k1), (p0, p1), (s0, s1) = (halves(o) for o in (Q, K, PR, SU))
                fq1, fk0 = halves(FQ)[1], halves(FK)[0]
                if lv >= 2:
                    pe_group(("A", tag, lv - 1, 1))
                v.tensor_tensor(fq1, q1, p1, ALU.mult)
                done(v.tensor_tensor(fk0, k0, s0, ALU.mult), ("F", tag, lv))
                mine(("F", tag, lv))
                if lv < 8:
                    link(v.tensor_tensor(s0, s0, p1[:, :, n - 1:n].broadcast_to([P, nb, n]), ALU.mult))
                    link(v.tensor_tensor(p1, p1, p0[:, :, n - 1:n].broadcast_to([P, nb, n]), ALU.mult))

            def scores_out(tag, lv):
                for t in range(TT):
                    pe_group(("A", tag, lv, t))
                    b = (6 if lv % 2 == 0 else 2) + t
                    plain(dve)
                    v.copy_predicated(attn[:, t, :, :],
                                      mask[:, lv:lv + 1, :].broadcast_to([P, HEADS, P]),
                                      ps[:, b, :].rearrange("p (h s) -> p h s", h=HEADS)).then_inc(emptied[b].sem, 1)

            def last_scores(tag):
                pe_group(("A", tag, 8, 0))
                v.tensor_copy(w(AX_, 512), ps[:, 6, :]).then_inc(emptied[6].sem, 1)
                dve.wait_ge(emptied[6].sem, emptied[6].at(("A", tag, 8, 0), 1))
                done(v.memset(small[:, 63:64], 0.0), ("attn", tag))

            for ins in (v.memset(ones[:], 1.0), v.memset(epsc[:, 0:1], LN_EPS), v.memset(epsc[:, 1:2], 1e-6),
                        v.memset(epsc[:, 2:3], 1.0), v.memset(wpool[:], 0.0), v.memset(w(AA, 1024), 0.0),
                        v.memset(w(FQ, 2048), 0.0), v.memset(w(UP, 516), 0.0), v.memset(w(PU, 544), 0.0)):
                pass
            done(ins, "zeros")
            dve.wait_ge(first.sem, 16 * 6)
            v.tensor_copy(mask[:].rearrange("p l t -> p (l t)"), w(V, 1024))
            bank_empty(0, "params")
            evac_T("x", dst=hT)
            evac_T("mem", dst=memT)
            la, lb_ = col("rec_lb", 0, 4), col("rec_lb", 4, 4)
            link(v.tensor_tensor(small[:, 48:52], la, lb_, ALU.max))
            v.tensor_tensor(small[:, 24:28], la, small[:, 48:52], ALU.subtract)
            done(v.tensor_tensor(small[:, 28:32], lb_, small[:, 48:52], ALU.subtract), "consts0")
            dve.wait_ge(act_done.sem, act_done.at("lbexp"))
            link(v.tensor_tensor(small[:, 52:56], small[:, 32:36], small[:, 36:40], ALU.add))
            link(v.reciprocal(small[:, 52:56], small[:, 52:56]))
            v.tensor_tensor(small[:, 32:36], small[:, 32:36], small[:, 52:56], ALU.mult)
            link(v.tensor_tensor(small[:, 36:40], small[:, 36:40], small[:, 52:56], ALU.mult))
            v.tensor_tensor(lbt[:, 0, 0:4], small[:, 32:36], small[:, 32:36], ALU.subtract)
            link(v.tensor_tensor(small[:, 56:60], small[:, 32:36], small[:, 36:40], ALU.add))
            link(v.tensor_tensor(lbt[:, 0, 4:8], small[:, 56:60], small[:, 32:36], ALU.subtract))
            v.tensor_scalar(lbt[:, 1, :], lbt[:, 0, :], -1.0, 1.0, ALU.mult, ALU.add)
            link(v.tensor_scalar(small[:, 40:48], col("lru_lambda_2", 0, 8), -1.0, 0.0, ALU.mult, ALU.max))
            link(v.tensor_tensor(small[:, 40:48], small[:, 40:48], small[:, 16:24], ALU.add))
            v.tensor_scalar(sp8[:, 0, :], small[:, 40:48], 8.0, None, ALU.mult)
            done(v.tensor_scalar(sp8[:, 1, :], small[:, 40:48], -8.0, None, ALU.mult), "consts")

            with counted(book, dve, "L", LAYERS, [dve_done]) as L:
                ffn("f1")
                ln(0, ("ln_g", "ln_b"), L * 32, ALPHA, lambda: slot_used(dve, key("f1", "down", 10)))
                for hd in range(HEADS):
                    if hd % 2 == 0:
                        bank_empty(hd // 2, f"rf{hd // 2}")
                    ins = v.tensor_scalar(pr[:, hd, :], work[:, FQ + hd * T:FQ + hd * T + T],
                                          lbt[:, 1, bass.ds(L * 4 + hd, 1)], lbt[:, 0, bass.ds(L * 4 + hd, 1)],
                                          ALU.mult, ALU.add)
                link(ins)
                v.memset(w(SU, 1024), 1.0)
                done(v.tensor_scalar(w(K, 1024), w(PR, 1024), -1.0, 1.0, ALU.mult, ALU.add), ("k", "r"))
                mine(("k", "r"))
                bank_empty(2, "rq0")
                bank_empty(3, "rq1")
                decay_step("r", 1)
                slot_used(dve, "ch")
                bank_empty(0, "cc")
                v.tensor_tensor(w(UP, 516, "p (g t) -> p g t", g=2)[:, :, 2:258],
                                ps[:, 1, :].rearrange("p (g t) -> p g t", g=2),
                                w(CC, 512, "p (g t) -> p g t", g=2), ALU.mult).then_inc(emptied[1].sem, 1)
                scores_out("r", 0)
                for lv in range(2, 9):
                    decay_step("r", lv)
                    scores_out("r", lv - 1)
                last_scores("r")
                for j in range(2):
                    dve.wait_ge(emptied[j].sem, emptied[j].at(("ms", "r", j), 1))
                    link(v.reciprocal(work[:, Q + 512 * j:Q + 512 * j + 512], work[:, Q + 512 * j:Q + 512 * j + 512]))
                    for uu in range(2):
                        u = 2 * j + uu
                        ins = v.scalar_tensor_tensor(out=work[:, FQ + u * T:FQ + u * T + T],
                                                     in0=ps[:, obank("r", j), uu * T:uu * T + T],
                                                     scalar=col("rec_norm_g", L * 4 + u),
                                                     in1=work[:, Q + u * T:Q + u * T + T], op0=ALU.mult, op1=ALU.mult)
                    ins.then_inc(emptied[obank("r", j)].sem, 1)
                    bank_empty(obank("r", j), ("O", "r", j))
                    bank_empty(j, f"rg{j}")
                    done(v.tensor_tensor(work[:, Y + 512 + 512 * j:Y + 1024 + 512 * j],
                                         work[:, Y + 512 + 512 * j:Y + 1024 + 512 * j],
                                         work[:, FQ + 512 * j:FQ + 512 * j + 512], ALU.mult), ("y", "r", j))
                ln(1, ("ln_g", "ln_b"), L * 32 + 8, ALPHA, lambda: slot_used(dve, "wo3"))

                def negmax(hd):
                    b = hd % 2
                    pe_group(("sc", hd))
                    link(v.tensor_reduce(smax[:, hd, :], ps[:, b, :].rearrange("p (t m) -> p t m", t=TT), AX.X, ALU.max))
                    done(v.tensor_scalar(smax[:, hd, :], smax[:, hd, :], -1.0 / 16, None, ALU.mult), ("nm", hd))

                def normalise(hd):
                    bank_empty(hd % 2, ("sc", hd))
                    link(v.reciprocal(ssum[:, hd, :], ssum[:, hd, :]))
                    for t in range(TT):
                        x = work[:, FQ + 512 * (hd % 2) + t * T:FQ + 512 * (hd % 2) + t * T + T]
                        ins = v.tensor_scalar(x, x, ssum[:, hd, t:t + 1], None, ALU.mult)
                    done(ins, ("p", hd))

                def o_copy(hd):
                    pe_group(("co", hd))
                    v.tensor_copy(work[:, PR + 512 * hd:PR + 512 * hd + 512], ps[:, 3, :]).then_inc(emptied[3].sem, 1)

                negmax(0)
                negmax(1)
                normalise(0)
                o_copy(0)
                normalise(1)
                negmax(2)
                o_copy(1)
                normalise(2)
                negmax(3)
                o_copy(2)
                normalise(3)
                o_copy(3)
                ln(2, ("ln_g", "ln_b"), L * 32 + 16, ALPHA, lambda: slot_used(dve, "co3"))
                ffn("f2")
                ln(3, ("ln_g", "ln_b"), L * 32 + 24, ALPHA, lambda: slot_used(dve, key("f2", "down", 10)))

            xa = w(XA, 2072, "p (g t) -> p g t", g=8)
            xc = w(XC, 2048, "p (g t) -> p g t", g=8)
            link(v.memset(xa[:, :, 0:3], 0.0))
            for g in range(8):
                if g % 2 == 0:
                    bank_empty(g // 2, f"xa{g // 2}")
                done(v.tensor_scalar(xc[:, g, :], xa[:, g, 0:T], col("conv_w_2", g), col("conv_b_2", g),
                                     ALU.mult, ALU.add), ("conv", g, 0))
            for k in range(1, 4):
                for g in range(8):
                    mine(("conv", g, k - 1))
                    ins = v.scalar_tensor_tensor(out=xc[:, g, :], in0=xa[:, g, k:k + T], scalar=col("conv_w_2", 8 * k + g),
                                                 in1=xc[:, g, :], op0=ALU.mult, op1=ALU.add)
                    done(ins, "xc" if (k, g) == (3, 7) else ("conv", g, k))
            for hd in range(HEADS):
                dve.wait_ge(act_done.sem, act_done.at(("zabs", hd // 2 * 2 + 1)))
                ins = v.tensor_scalar(su[:, hd, :], ps[:, hd // 2, (hd % 2) * T:(hd % 2) * T + T],
                                      col("gla_b_gate_2", hd), 0.0, ALU.add, ALU.min)
                if hd % 2:
                    ins.then_inc(emptied[hd // 2].sem, 1)
            bank_empty(1, ("zg", 1))
            dve.wait_ge(act_done.sem, act_done.at("zln"))
            done(v.tensor_tensor(w(SU, 1024), w(SU, 1024), w(PR, 1024), ALU.subtract), "logsig")
            dve.wait_ge(act_done.sem, act_done.at("decay"))
            v.memset(w(SU, 1024), 1.0)
            dve.wait_ge(act_done.sem, act_done.at("tanh"))
            link(v.tensor_scalar(w(Y, 2048), w(TH, 2048), 1.0, None, ALU.add))
            link(v.reciprocal(w(Y, 2048), w(Y, 2048)))
            done(v.tensor_tensor(w(TH, 2048), w(TH, 2048), w(Y, 2048), ALU.mult), "ratio")
            dve.wait_ge(act_done.sem, act_done.at("mult"))
            dve.wait_ge(pool_done.sem, pool_done.at("ix"))
            v.memset(w(R, 2048, "p (g t) -> p g t", g=8)[:, :, 0:1], 0.0)
            link(v.tensor_tensor(w(IG, 2048), w(IG, 2048), w(TH, 2048), ALU.mult))
            done(v.tensor_tensor_scan(w(XC, 2048), w(R, 2048), w(IG, 2048), 0.0, ALU.mult, ALU.add), "scan")
            for j in range(2):
                bank_empty(j, f"q{j}")
                bank_empty(2 + j, f"k{j}")
            decay_step("g", 1)
            scores_out("g", 0)
            for lv in range(2, 6):
                decay_step("g", lv)
                scores_out("g", lv - 1)

            def times(nm, j):
                bank_empty(j % 2, f"{nm}{j}")
                x = work[:, XC + 512 * j:XC + 512 * j + 512]
                done(v.tensor_tensor(x, x, work[:, R + 512 * (j % 2):R + 512 * (j % 2) + 512], ALU.mult), (nm, j))

            mine("scan")
            for lv in range(6, 9):
                times("ga", lv - 6)
                decay_step("g", lv)
                scores_out("g", lv - 1)
            times("ga", 3)
            last_scores("g")
            for j in range(4):
                mine(("ga", j))
                times("ma", j)
            dve.wait_ge(pool_done.sem, pool_done.at(("mb", 3)))
            for j in range(2):
                bank_empty(j, ("ms", "g", j))
                link(v.reciprocal(work[:, Q + 512 * j:Q + 512 * j + 512], work[:, Q + 512 * j:Q + 512 * j + 512]))
            for j in range(4):
                for uu in range(2):
                    u = 2 * j + uu
                    ins = v.scalar_tensor_tensor(out=work[:, FQ + u * T:FQ + u * T + T],
                                                 in0=ps[:, obank("g", j), uu * T:uu * T + T],
                                                 scalar=col("gla_norm_g_2", uu), in1=work[:, Q + j * T:Q + j * T + T],
                                                 op0=ALU.mult, op1=ALU.mult)
                ins.then_inc(emptied[obank("g", j)].sem, 1)
                bank_empty(obank("g", j), ("O", "g", j))
                x = work[:, FQ + 512 * j:FQ + 512 * j + 512]
                link(v.tensor_tensor(x, x, hn[:].rearrange("p t n -> p (t n)")[:, 512 * j:512 * j + 512], ALU.mult))
                mine(("ma", j))
                done(v.tensor_tensor(work[:, Y + 512 * j:Y + 512 * j + 512], x,
                                     work[:, XC + 512 * j:XC + 512 * j + 512], ALU.add), ("y", "g", j))
            ln("A", ("ln1_g_2", "ln1_b_2"), 0, ALPHA2, lambda: slot_used(dve, "w2o3"))

            slot_used(dve, "router")
            v.tensor_copy(work[:, LOGIT:LOGIT + 64], ps[:, 0, 0:64]).then_inc(emptied[0].sem, 1)
            bank_empty(0, "router")
            lg = w(LOGIT, 64, "p (t e) -> p t e", t=TT)
            link(v.tensor_reduce(small[:, 40:42], lg, AX.X, ALU.max))
            done(v.tensor_scalar(small[:, 40:42], small[:, 40:42], -1.0, None, ALU.mult), "rmax")
            s = slot_of["tri"]
            dve.wait_ge(loaded[s].sem, loaded[s].at("tri"))
            for t in range(TT):
                li = lg[:, t:t + 1, :].broadcast_to([P, 32, 32])
                lj = w(LOGIT + 32 * t, 32).rearrange("p (e o) -> p e o", o=1).broadcast_to([P, 32, 32])
                gt = w(CMP, 1024, "p (j i) -> p j i", j=32)
                eq = w(CMP + 1024, 1024, "p (j i) -> p j i", j=32)
                v.tensor_tensor(gt, li, lj, ALU.is_gt)
                link(v.tensor_tensor(eq, li, lj, ALU.is_equal))
                link(v.tensor_tensor(w(CMP + 1024, 1024), w(CMP + 1024, 1024), ring[:, s, 0:1024], ALU.mult))
                link(v.tensor_tensor(w(CMP, 1024), w(CMP, 1024), w(CMP + 1024, 1024), ALU.add))
                link(v.tensor_reduce(work[:, RANK + 32 * t:RANK + 32 * t + 32], gt, AX.X, ALU.add))
            link(v.tensor_scalar(w(RANK, 64), w(RANK, 64), float(TOPK), None, ALU.is_lt))
            v.memset(small[:, 60:61], 0.0).then_inc(used[s].sem, 1)
            dve.wait_ge(act_done.sem, act_done.at("rexp"))
            link(v.tensor_tensor(w(GATES, 64), w(GATES, 64), w(RANK, 64), ALU.mult))
            link(v.tensor_reduce(small[:, 42:44], w(GATES, 64, "p (t e) -> p t e", t=TT), AX.X, ALU.add))
            link(v.reciprocal(small[:, 42:44], small[:, 42:44]))
            for t in range(TT):
                x = work[:, GATES + 32 * t:GATES + 32 * t + 32]
                ins = v.tensor_scalar(x, x, small[:, 42 + t:43 + t], None, ALU.mult)
            done(ins, "gates")
            slot_used(dve, "bdown")
            for b in range(4, 8):
                v.tensor_copy(work[:, MACC + 512 * (b - 4):MACC + 512 * (b - 4) + 512], ps[:, b, :])\
                    .then_inc(emptied[b].sem, 1)
            for b in range(4, 8):
                bank_empty(b, "bd")
            bank_empty(1, "bup")
            with counted(book, dve, "e", EXPERTS, [dve_done]) as e:
                def swish(j):
                    g, b = 2 * (j % 2), 512 * (j % 2)
                    slot_used(dve, ("moe", "g", j))
                    for kk in range(2):
                        ins = v.tensor_scalar(work[:, GH + b + kk * T:GH + b + kk * T + T], ps[:, g, kk * T:kk * T + T],
                                              work[:, bass.ds(e * 16 + (BUP + 2 * j + kk), 1)], LIMIT, ALU.add, ALU.min)
                    ins.then_inc(emptied[g].sem, 1)
                    slot_used(dve, ("moe", "u", j))
                    for kk in range(2):
                        ins = v.tensor_scalar(work[:, UH + b + kk * T:UH + b + kk * T + T], ps[:, g + 1, kk * T:kk * T + T],
                                              work[:, bass.ds(e * 16 + (BUP + 8 + 2 * j + kk), 1)], LIMIT, ALU.add, ALU.min)
                    ins.then_inc(emptied[g + 1].sem, 1)
                    bank_empty(g + 1, ("moe", "u", j))
                    uh, gh, sg = (work[:, o + b:o + b + 512] for o in (UH, GH, SG))
                    link(v.tensor_scalar(uh, uh, -LIMIT, 1.0, ALU.max, ALU.add))
                    bank_empty(g, ("moe", "g", j))
                    link(v.tensor_tensor(uh, uh, gh, ALU.mult))
                    dve.wait_ge(act_done.sem, act_done.at(("sg", j)))
                    done(v.tensor_tensor(work[:, ACTT + 512 * j:ACTT + 512 * j + 512], uh, sg, ALU.mult), ("act", j))

                for j in range(4):
                    swish(j)
                slot_used(dve, ("moe", "d", 3))
                for t in range(TT):
                    for half in range(2):
                        b = 4 + 2 * t + half
                        x = work[:, MACC + t * D + half * 512:MACC + t * D + half * 512 + 512]
                        v.scalar_tensor_tensor(out=x, in0=ps[:, b, :], scalar=work[:, bass.ds(e + (GATES + 32 * t), 1)],
                                               in1=x, op0=ALU.mult, op1=ALU.add).then_inc(emptied[b].sem, 1)
                for b in range(4, 8):
                    bank_empty(b, "moe")
            ln("B", ("ln2_g_2", "ln2_b_2"), 0, ALPHA2, lambda: None, banked=False)
            slot_used(dve, "wple")
            dve.wait_ge(h_ready.sem, h_ready.at(("h", "B")))
            for t in range(TT):
                for half in range(2):
                    b = 2 * t + half
                    bank_empty(4 + b, "pg")
                    x = hn[:, t, half * 512:half * 512 + 512]
                    v.tensor_tensor(x, x, ps[:, b, :], ALU.mult).then_inc(emptied[b].sem, 1)
                bank_empty(2 * t, "ple")
                bank_empty(2 * t + 1, "ple")
                done(v.tensor_tensor(h[:, t, :], h[:, t, :], hn[:, t, :], ALU.add), ("out", t))

        @block.gpsimd
        def _(pool):
            g = nc.gpsimd

            def done(ins, name):
                ins.then_inc(pool_done.add(name), 1)

            def link(ins):
                name = ("link", pool_done.n, tuple(pool_done.loops))
                ins.then_inc(pool_done.add(name), 1)
                pool.wait_ge(pool_done.sem, pool_done.at(name))
                plain(pool)

            def residual(tag):
                name = ("lnp", tag)
                s = slot_of[name]
                pool.wait_ge(loaded[s].sem, loaded[s].at(name))
                for t in range(TT):
                    pool.wait_ge(dve_done.sem, dve_done.at(("hn", tag, t)))
                    link(g.tensor_tensor(h[:, t, :], hn[:, t, :], ring[:, s, 0:D], ALU.mult))
                    ins = g.tensor_tensor(h[:, t, :], h[:, t, :], ring[:, s, D:2 * D], ALU.add)
                    if t == 1:
                        ins.then_inc(h_ready.add(("h", tag)), 1)
                pool.wait_ge(h_ready.sem, h_ready.at(("h", tag)))
                pool.sem_inc(used[s].sem, 1)

            pool.wait_ge(first.sem, 16 * 6)
            pool.sem_inc(h_ready.add("x"), 1)
            pool.wait_ge(dve_done.sem, dve_done.at("zeros"))
            with counted(book, pool, "L", LAYERS, [pool_done, h_ready]) as L:
                residual(0)
                up = w(UP, 516, "p (g t) -> p g t", g=2)
                tc = w(TC, T)
                pool.wait_ge(emptied[1].sem, emptied[1].at("ch", 1))
                pool.wait_ge(emptied[0].sem, emptied[0].at("cb", 1))
                plain(pool)
                link(g.tensor_copy(taps[:], cols[:, 1, bass.ds(L * 6 + 16, 6)]))
                for ct in range(2):
                    y = yT[:, ct, :]
                    link(g.tensor_scalar(y, up[:, ct, 0:T], taps[:, ct:ct + 1], None, ALU.mult))
                    for k in range(1, 3):
                        link(g.tensor_scalar(tc, up[:, ct, k:k + T], taps[:, 2 * k + ct:2 * k + ct + 1], None, ALU.mult))
                        link(g.tensor_tensor(y, y, tc, ALU.add))
                    ins = g.tensor_tensor(y, y, work[:, CC + ct * T:CC + ct * T + T], ALU.mult)
                done(ins, "conv")
                pu, sa, sbb = (w(o, 544, "p (g t) -> p g t", g=2) for o in (PU, SA, SB))
                pm = w(PM, 512, "p (g t) -> p g t", g=2)
                pool.wait_ge(emptied[1].sem, emptied[1].at("pu", 1))
                link(g.tensor_tensor(sa[:, :, 1:272], pu[:, :, 1:272], pu[:, :, 0:271], ALU.add))
                link(g.tensor_tensor(sbb[:, :, 3:272], sa[:, :, 3:272], sa[:, :, 1:270], ALU.add))

                def mean(x, lo, kt):
                    link(g.tensor_scalar(pm[lo:lo + 64, kt, :], x[lo:lo + 64, kt, 16:272], cnt[lo:lo + 64, kt, 16:17],
                                         None, ALU.mult))
                    link(g.tensor_tensor(pm[lo:lo + 64, kt, 0:16], x[lo:lo + 64, kt, 16:32], cnt[lo:lo + 64, kt, 0:16],
                                         ALU.mult))

                mean(sa, 0, 0)
                mean(sbb, 64, 0)
                link(g.tensor_tensor(sa[:, 1, 7:272], sbb[:, 1, 7:272], sbb[:, 1, 3:268], ALU.add))
                link(g.tensor_tensor(sbb[:, 1, 15:272], sa[:, 1, 15:272], sa[:, 1, 7:264], ALU.add))
                mean(sa, 0, 1)
                mean(sbb, 64, 1)
                done(g.tensor_tensor(pm, pm, pu[:, :, 16:272], ALU.subtract), "pooled")
                residual(1)
                residual(2)
                residual(3)
            pool.wait_ge(emptied[3].sem, emptied[3].at(("lru", "i", 3), 1))
            pool.wait_ge(dve_done.sem, dve_done.at("xc"))
            done(g.tensor_tensor(w(IG, 2048), w(IG, 2048), w(XC, 2048), ALU.mult), "ix")
            gob = hn[:].rearrange("p t n -> p (t n)")
            for j in range(4):
                pool.wait_ge(emptied[j % 2].sem, emptied[j % 2].at(f"mb{j}", 1))
                x = gob[:, 512 * j:512 * j + 512]
                done(g.tensor_tensor(x, x, work[:, TH + 512 * (j % 2):TH + 512 * (j % 2) + 512], ALU.mult), ("mb", j))
            residual("A")
            residual("B")


LOGIT, RANK, GATES, GT, CMP = 0, 64, 128, 192, 1024
BUP, GH, UH, SG = 3072, 6144, 7168, 8192
ACTT, MACC = 9728, 11776

_SHAPES = {}
_INS = ['x', 'mem', 'ffn1_gate', 'ffn1_up', 'ffn1_down', 'w_in', 'conv_w', 'rec_lb', 'rec_norm_g', 'pool_w',
        'pool_scale', 'w_out', 'ca_q', 'ca_k', 'ca_v', 'ca_o', 'ffn2_gate', 'ffn2_up', 'ffn2_down', 'ln_g', 'ln_b',
        'p_2', 'w_in_2', 'conv_w_2', 'conv_b_2', 'lru_w_r_2', 'lru_b_r_2', 'lru_w_i_2', 'lru_b_i_2', 'lru_lambda_2',
        'gla_w_gate_2', 'gla_b_gate_2', 'gla_norm_g_2', 'w_out_2', 'ln1_g_2', 'ln1_b_2', 'w_router_2', 'b_router_2',
        'w_up_2', 'b_up_2', 'w_down_2', 'b_down_2', 'ln2_g_2', 'ln2_b_2', 'w_ple_2', 'w_ple_gate_2', 'b_ple_gate_2']


def constants():
    s, t = np.arange(P)[:, None], np.arange(P)[None, :]
    apart = s ^ t
    mask = np.zeros((P, 8, P), np.float32)
    mask[:, 0] = s == t
    for lv in range(1, 8):
        mask[:, lv] = (t > s) & (apart >> (lv - 1) == 1)
    window = np.array([[2, 8], [4, 16]])[np.arange(P) // 64]
    count = np.minimum(np.arange(17) + 1, window[:, :, None])
    count[:, :, 16] = window
    tri = np.broadcast_to((np.arange(32)[None, :] < np.arange(32)[:, None]).reshape(1, 1024), (P, 1024))
    return {"c_ident": np.eye(P, dtype=np.float32), "c_mask": mask,
            "c_cnt": (1.0 / count).astype(np.float32), "c_tri": np.ascontiguousarray(tri, dtype=np.float32)}


def kernel(**inputs):
    import concourse.bacc as _bacc
    from concourse.bass_utils import run_bass_kernel_spmd as _run

    arrays = {n: np.ascontiguousarray(inputs[n]) for n in _INS}
    arrays.update(constants())
    book = Book()
    for _ in range(2):
        nc = _bacc.Bacc("TRN2", target_bir_lowering=False, num_devices=1)
        a = {n: nc.dram_tensor(f"in_{n}_dram", v.shape, mybir.dt.from_np(v.dtype), kind="ExternalInput").ap()
             for n, v in arrays.items()}
        a["out"] = nc.dram_tensor("out_0_dram", (1, T, D), F32, kind="ExternalOutput").ap()
        program(nc, book, a)
        book.turn()
    r = _run(nc, [{f"in_{n}_dram": v for n, v in arrays.items()}], core_ids=[0])
    return r.results[0]["out_0_dram"]
```

```python
from contextlib import ExitStack, contextmanager

import numpy as np
import concourse.bass as bass
from concourse import mybir

F32 = mybir.dt.float32
F32R = mybir.dt.float32r
U8 = mybir.dt.uint8
ALU = mybir.AluOpType
ACT = mybir.ActivationFunctionType
AX = mybir.AxisListType

P = 128
T = 256
TT = T // P
D = 1024
DT = D // P
LAYERS = 2
FF = 2816
CH = 256
NCH = FF // CH
RING = 12
SLOT = 2048
ALPHA = (2.0 * LAYERS) ** 0.25
ALPHA2 = 2.0 ** 0.25
LN_EPS = 1e-5
HEADS = 4
LEVELS = 9
EXPERTS = 32
TOPK = 4
LIMIT = 7.0
CAP = 64
SIG_ALPHA = 1.702

COLS1 = [("ln_g", 64), ("ln_b", 64)]
COLS2 = [("rec_lb", 8), ("rec_norm_g", 8), ("conv_w", 12), ("pool_scale", 4), ("conv_w_2", 32),
         ("conv_b_2", 8), ("lru_b_r_2", 8), ("lru_b_i_2", 8), ("lru_lambda_2", 8),
         ("gla_b_gate_2", 4), ("gla_norm_g_2", 2)]
COLS3 = [("ln1_g_2", 8), ("ln1_b_2", 8), ("ln2_g_2", 8), ("ln2_b_2", 8)]

Q, K, PR, SU, FQ, FK, AA, AX_, V, Y = 0, 1024, 2048, 3072, 4096, 5120, 6144, 7168, 7680, 9728
MEMT, KT, VM, CC, UP = 11776, 13824, 15872, 17920, 18432
PU, SA, SB, PM, TC = 8704, 18948, 19492, 20036, 20548
XC, XA, R, IG, TH = 11776, 13824, 13824, 15904, 17952
WORK = 20804
GH_, UH_, DH_, HTH, HTL, HDH, HDL = KT, VM, Q, PR, Y, V, 18952
NORM_OF = {"f1": 0, "f2": 3}


class Book:

    def __init__(self):
        self.place, self.per = {}, {}
        self.old_place, self.old_per = None, None
        self.slots = {}
        self.iters = {}

    def turn(self):
        self.old_place, self.old_per = self.place, self.per
        self.place, self.per = {}, {}


class Line:

    def __init__(self, book, sem, key, unit=1):
        self.book, self.sem, self.key, self.unit = book, sem, key, unit
        self.n, self.loops = 0, []

    def add(self, name):
        self.n += 1
        assert (self.key, name) not in self.book.place, (self.key, name)
        self.book.place[self.key, name] = (self.n, tuple(self.loops))
        return self.sem

    def at(self, name, plus=0, **iters):
        if self.book.old_place is None:
            return 1
        n, loops = self.book.old_place[self.key, name]
        v = plus + n
        for loop in loops:
            per = self.book.old_per[self.key, loop]
            it = iters[loop] if loop in iters else self.book.iters[loop]
            if per and not (isinstance(it, int) and it == 0):
                v = v + it * per
        return v * self.unit


@contextmanager
def counted(book, eng, name, n, lines, also=None):
    start = [ln.n for ln in lines]
    for ln in lines:
        ln.loops.append(name)
    with eng.Fori(0, n) as it:
        book.iters[name] = it
        if also:
            book.iters[also] = it
        yield it
    del book.iters[name]
    for ln, s in zip(lines, start):
        ln.loops.pop()
        ln.book.per[ln.key, name] = ln.n - s
        ln.n = s + (ln.n - s) * n


class Fork:

    def __init__(self, book, eng, name, lines):
        self.book, self.eng, self.name, self.lines = book, eng, name, lines
        self.start = [ln.n for ln in lines]
        self.most = list(self.start)

    def end(self, branch, offset):
        for i, ln in enumerate(self.lines):
            self.book.place[ln.key, (self.name, branch)] = (ln.n, ())
            if self.book.old_place is not None:
                ends = [self.book.old_place[ln.key, (self.name, b)][0] for b in ("few", "many")]
                if max(ends) > ln.n:
                    if ln.n > self.start[i]:
                        self.eng.wait_ge(ln.sem, ln.n + offset[i])
                    self.eng.sem_inc(ln.sem, max(ends) - ln.n)
            self.most[i] = max(self.most[i], ln.n)
            ln.n = self.start[i]

    def join(self):
        for ln, n in zip(self.lines, self.most):
            ln.n = n


def program(nc, book, a):
    book.iters = {}
    with ExitStack() as ctx:
        def sb(name, shape, dt=F32):
            return ctx.enter_context(nc.sbuf_tensor(name, shape, dt))

        def line(name, unit=1):
            return Line(book, ctx.enter_context(nc.semaphore(name)), name, unit)

        with nc.sbuf_tensor("ring", [P, RING, SLOT], F32) as ring, nc.sbuf_tensor("work", [P, WORK], F32) as work:
            pass
        ring_halves = [sb(f"ring_halves{i}", [P, SLOT], F32R) for i in range(RING)]
        work_halves, at = {}, 0
        for off, size in sorted(((DH_, 2048), (HTH, 2048), (HDL, 1024), (HDH, 1024), (HTL, 2048), (GH_, 2048), (UH_, 2048))):
            if off > at:
                sb(f"between{off}", [P, off - at])
            work_halves[off] = sb(f"work_halves{off}", [P, size], F32R)
            at = off + size
        sb("after_halves", [P, WORK - at])
        h = sb("h", [P, TT, D])
        hn = sb("hn", [P, TT, D])
        hT = sb("hT", [P, DT, T])
        ident = sb("ident", [P, P])
        ones = sb("ones", [P, P])
        mask = sb("mask", [P, 8, P], U8)
        cols = sb("cols", [P, 3, P])
        cnt = sb("cnt", [P, 2, 17])
        wpool = sb("wpool", [P, 2, P])
        lbt = sb("lbt", [P, 2, 8])
        sp8 = sb("sp8", [P, 2, 8])
        stat = sb("stat", [P, TT, 2, 6])
        mv = sb("mv", [P, TT, 2])
        rstd = sb("rstd", [P, TT])
        small = sb("small", [P, 64])
        most = sb("most", [P, 1], mybir.dt.int32)
        taps = sb("taps", [P, 6])
        epsc = sb("epsc", [P, 3])
        smax = sb("smax", [P, HEADS, TT])
        ssum = sb("ssum", [P, HEADS, TT])
        brout = sb("brout", [1, 32])
        ps = ctx.enter_context(nc.psum_tensor("ps", [P, 8, 512], F32))

        loaded = [line(f"loaded{s}", 16) for s in range(RING)]
        used = [line(f"used{s}") for s in range(RING)]
        emptied = [line(f"emptied{b}") for b in range(8)]
        pe_full = line("pe_full")
        act_done = line("act_done")
        dve_done = line("dve_done")
        pool_done = line("pool_done")
        hi_done = line("hi_done")
        lo_done = line("lo_done")
        sel_ready = line("sel_ready")
        h_ready = line("h_ready")
        first = line("first_loads", 16)
        prm = line("param_loads", 16)
        out_done = line("out_done", 16)
        passed = ctx.enter_context(nc.semaphore("passed"))

        slot_of = book.slots

        def w(off, size, shape=None, **kw):
            v = work[:, off:off + size]
            return v.rearrange(shape, **kw) if shape else v

        qT = w(Q, 1024, "p (g t) -> p g t", g=4)
        kT_ = w(K, 1024, "p (g t) -> p g t", g=4)
        pr = w(PR, 1024, "p (g t) -> p g t", g=4)
        su = w(SU, 1024, "p (g t) -> p g t", g=4)
        fq = w(FQ, 1024)
        fk = w(FK, 1024)
        attn = w(AA, 1024, "p (t h s) -> p t h s", t=TT, h=HEADS)
        cross = w(AX_, 512, "p (h s) -> p h s", h=HEADS)
        yT = w(Y, 2048, "p (g t) -> p g t", g=8)
        memT = w(MEMT, 2048, "p (g t) -> p g t", g=8)
        keyT = w(KT, 2048, "p (g t) -> p g t", g=8)
        valm = w(VM, 2048, "p (t n) -> p t n", t=TT)

        def wr(off, size):
            base = max(o for o in work_halves if o <= off)
            return work_halves[base][:, off - base:off - base + size]

        def chunk_event(line_, tag, what, c, i=None):
            n = {"gate": 3 * c - 3, "up": 3 * c - 2, "down": 3 * c + 2}[what]
            if (what, c) == ("down", 10):
                n = 30
            return line_.at((tag, "gate", 1), n if i is None else i * 12 + n)

        def col(name, i, n=1):
            for b, group in enumerate((COLS1, COLS2, COLS3)):
                at = 0
                for nm, rows in group:
                    if nm == name:
                        if isinstance(i, int):
                            return cols[:, b, at + i:at + i + n]
                        return cols[:, b, bass.ds(i + at, n)]
                    at += rows

        def key(tag, what, c):
            return (tag, what, c)

        def obank(tag, j):
            return (2, 3)[j] if tag == "r" else (2, 3, 4, 5)[j]

        def slot_used(eng, name, plus=0, **iters):
            s = slot_of[name]
            eng.wait_ge(used[s].sem, used[s].at(name, plus + 1, **iters))

        def plain(eng):
            eng.sem_inc(passed, 1)

        block = ctx.enter_context(nc.Block())

        @block.sync
        def _(sp):
            def once(dst, src):
                sp.dma_start(dst, src).then_inc(first.add(first.n), 16)

            once(ident[:], a["c_ident"])
            once(h[:], a["x"].rearrange("a (t p) n -> p (a t) n", p=P))
            once(w(KT, 2048, "p (t n) -> p t n", t=TT), a["mem"].rearrange("a (t p) n -> p (a t) n", p=P))
            once(w(V, 1024), a["c_mask"].rearrange("p l t -> p (l t)"))
            once(cnt[:], a["c_cnt"])
            once(brout[:], a["b_router_2"])
            pos = [0]
            sp.wait_ge(first.sem, 16 * 6)

            def load(name, src, shape, part=P, **kw):
                s = pos[0] % RING
                pos[0] += 1
                used[s].add(name)
                loaded[s].add(name)
                slot_of[name] = s
                n = 1
                for x in src.shape[1:]:
                    n *= x
                dst = ring[0:part, s, 0:n]
                if shape:
                    dst = dst.rearrange(shape, **kw)
                sp.wait_ge(used[s].sem, used[s].at(name))
                plain(sp)
                sp.dma_start(dst, src).then_inc(loaded[s].sem, 16)

            def align():
                pos[0] = -(-pos[0] // RING) * RING

            def columns(wt, c0):
                return wt.rearrange("(k p) n -> p k n", p=P)[:, :, c0:c0 + CH]

            def rows(wt, k0, n=2):
                return wt.rearrange("(k p) n -> p k n", p=P)[:, k0:k0 + n, :]

            def ln_params(name, g, b, i):
                s = pos[0] % RING
                pos[0] += 1
                used[s].add(name)
                loaded[s].add(name + ("g",))
                loaded[s].add(name)
                slot_of[name] = s
                sp.wait_ge(used[s].sem, used[s].at(name))
                plain(sp)
                for half, x in enumerate((g, b)):
                    sp.dma_start(ring[:, s, half * D:half * D + D],
                                 x[bass.ds(i, 1) if not isinstance(i, int) else slice(i, i + 1), :]
                                 .to_broadcast([P, D])).then_inc(loaded[s].sem, 16)

            def ffn(tag, wg, wu, wd, L):
                g = wg.rearrange("l (k p) n -> p l k n", p=P)
                u = wu.rearrange("l (k p) n -> p l k n", p=P)
                d = wd.rearrange("l (k p) n -> p l k n", p=P)

                def chunk(c, i=None):
                    n0 = bass.ds(i * (4 * CH) + c * CH, CH) if i is not None else slice(c * CH, c * CH + CH)
                    k0 = bass.ds(i * 8 + 2 * c, 2) if i is not None else slice(2 * c, 2 * c + 2)
                    load(key(tag, "gate", c), g[:, L, :, n0], "p (k n) -> p k n", k=DT)
                    load(key(tag, "up", c), u[:, L, :, n0], "p (k n) -> p k n", k=DT)
                    load(key(tag, "down", c), d[:, L, k0, :], "p (k n) -> p k n", k=2)

                chunk(0)
                chunk(1)
                with counted(book, sp, "c" + tag, 2, loaded + used) as i:
                    for c in range(2, 6):
                        chunk(c, i)
                pos[0] += 12
                chunk(10)

            with counted(book, sp, "L", LAYERS, loaded + used) as L:
                def wl(nm):
                    return a[nm].rearrange("l (k p) n -> p l k n", p=P)

                ffn("f1", a["ffn1_gate"], a["ffn1_up"], a["ffn1_down"], L)
                lng, lnb = (a[x].rearrange("l j n -> (l j) n") for x in ("ln_g", "ln_b"))
                ln_params(("lnp", 0), lng, lnb, L * 4)
                align()
                win = wl("w_in")

                def win_cols(name, c0):
                    load(name, win[:, L, :, c0:c0 + CH], "p (k n) -> p k n", k=DT)

                def full_cols(name, nm, c0):
                    load(name, wl(nm)[:, L, :, c0:c0 + CH], "p (k n) -> p k n", k=DT)

                def full_rows(name, nm, k0):
                    load(name, wl(nm)[:, L, k0:k0 + 2, :], "p (k n) -> p k n", k=2)

                for name, c0 in (("rf0", 1280), ("rf1", 1536), ("rq0", 768), ("rq1", 1024), ("cc", 256),
                                 ("ch", 512), ("cb", 0), ("pu", 2816)):
                    win_cols(name, c0)
                for j in range(2):
                    load(f"ri{j}", win[:, L, 4 * j:4 * j + 4, 1792:2304], "p (k n) -> p k n", k=4)
                for j in range(4):
                    full_cols(f"ck{j}", "ca_k", CH * j)
                for j in range(4):
                    full_rows(f"cv{j}", "ca_v", 2 * j)
                win_cols("rg0", 2304)
                win_cols("rg1", 2560)
                for j, k0 in enumerate((0, 6, 2, 4)):
                    full_rows(f"wo{j}", "w_out", k0)
                ln_params(("lnp", 1), lng, lnb, L * 4 + 1)
                for j in range(4):
                    full_cols(f"cq{j}", "ca_q", CH * j)
                for j in range(4):
                    full_rows(f"co{j}", "ca_o", 2 * j)
                ln_params(("lnp", 2), lng, lnb, L * 4 + 2)
                align()
                ffn("f2", a["ffn2_gate"], a["ffn2_up"], a["ffn2_down"], L)
                ln_params(("lnp", 3), lng, lnb, L * 4 + 3)
                align()

            win2 = a["w_in_2"].rearrange("a k n -> (a k) n")

            def cols2(name, c0):
                load(name, columns(win2, c0), "p (k n) -> p k n", k=DT)

            for j in range(4):
                cols2(f"xa{j}", CH * j)
            for j in range(2):
                cols2(f"q{j}", 2048 + CH * j)
            for j in range(2):
                cols2(f"k{j}", 2560 + CH * j)
            load("glr", win2.rearrange("(k p) n -> p k n", p=P)[:, :, 5120:5136], "p (k n) -> p k n", k=DT)
            load("glg", a["gla_w_gate_2"].rearrange("a r n -> (a r) n"), None, part=16)
            for j in range(4):
                load(f"v{j}", win2.rearrange("(k p) n -> p k n", p=P)[:, 2 * j:2 * j + 2, 3072:4096],
                     "p (k n) -> p k n", k=2)
            load("lrur", a["lru_w_r_2"].rearrange("a g c d -> c (a g) d"), "p (g d) -> p g d", g=8)
            load("lrui", a["lru_w_i_2"].rearrange("a g c d -> c (a g) d"), "p (g d) -> p g d", g=8)
            for j in range(4):
                cols2(f"go{j}", 4096 + CH * j)
            for j in range(4):
                cols2(f"mb{j}", 6160 + CH * j)
            for j in range(4):
                cols2(f"ga{j}", 1024 + CH * j)
            for j in range(4):
                cols2(f"ma{j}", 5136 + CH * j)
            wout2 = a["w_out_2"].rearrange("a k n -> (a k) n")
            for j in range(4):
                load(f"w2o{j}", rows(wout2, 2 * j), "p (k n) -> p k n", k=2)
            ln_params(("lnp", "A"), a["ln1_g_2"], a["ln1_b_2"], 0)
            load("router", a["w_router_2"].rearrange("a (k p) n -> p (a k) n", p=P), "p (k n) -> p k n", k=DT)
            load("tri", a["c_tri"], None)
            load("before", a["c_moe"].rearrange("p a n -> p (a n)"), None)
            load("bup", a["b_up_2"].rearrange("a e (j n) -> (a e j) n", n=P)
                 .rearrange("(b p) n -> p b n", p=P), "p (b n) -> p b n", b=4)
            load("bdown", a["b_down_2"].rearrange("a e n -> (a e) n"), None, part=32)
            align()
            wup = a["w_up_2"].rearrange("a e (k p) n -> p (a e) k n", p=P)
            wdn = a["w_down_2"].rearrange("a e (k p) n -> p (a e) k n", p=P)
            with counted(book, sp, "e", EXPERTS, loaded + used) as e:
                for what, j in [(x, j) for j in range(4) for x in "gu"] + [("d", j) for j in range(4)]:
                    if what == "d":
                        load(("moe", what, j), wdn[:, e, 2 * j:2 * j + 2, :], "p (k n) -> p k n", k=2)
                    else:
                        c0 = CH * j + (D if what == "u" else 0)
                        load(("moe", what, j), wup[:, e, :, c0:c0 + CH], "p (k n) -> p k n", k=DT)
            ln_params(("lnp", "B"), a["ln2_g_2"], a["ln2_b_2"], 0)
            load("ptok", a["p_2"].rearrange("l a (t p) n -> p (l a t) n", p=P), "p (t n) -> p t n", t=TT)
            load("wple", rows(a["w_ple_2"].rearrange("a k n -> (a k) n"), 0), "p (k n) -> p k n", k=2)
            load("bpg", a["b_ple_gate_2"], None, part=1)
            wpg = a["w_ple_gate_2"].rearrange("a k n -> (a k) n")
            for j in range(4):
                load(f"pg{j}", rows(wpg, 2 * j), "p (k n) -> p k n", k=2)

        @block.tensor
        def _(pe):
            for s in range(RING):
                pe.sem_inc(used[s].sem, 1)
            for b in range(8):
                pe.sem_inc(emptied[b].sem, 1)

            def open_bank(b, name):
                emptied[b].add(name)
                pe.wait_ge(emptied[b].sem, emptied[b].at(name))

            def arrived(name, plus=0):
                s = slot_of[name]
                pe.wait_ge(loaded[s].sem, loaded[s].at(name, plus))
                return s

            def by_columns(name, bank, x, content=None):
                open_bank(bank, content or name)
                s = arrived(name)
                for pt in range(2):
                    for k in range(DT):
                        mm = pe.matmul(ps[:, bank, pt * T:pt * T + T],
                                       ring[:, s, k * CH + pt * P:k * CH + pt * P + P], x[:, k, :],
                                       start=(k == 0), stop=(k == DT - 1))
                mm.then_inc(used[s].sem, 1)

            def by_rows(name, lhs, is_first, is_last, plus=0):
                s = arrived(name, plus)
                for kk in range(2):
                    for t in range(TT):
                        for half in range(2):
                            mm = pe.matmul(ps[:, 4 + 2 * t + half, :], lhs(kk, t),
                                           ring[:, s, kk * D + half * 512:kk * D + half * 512 + 512],
                                           start=(is_first and kk == 0), stop=(is_last and kk == 1))
                mm.then_inc(used[s].sem, 1)

            def last_rows(tag, pair):
                slots = []
                for t in range(TT):
                    for i, (name, lhs, ready) in enumerate(pair):
                        if t == 0:
                            ready()
                            s = slot_of[name]
                            pe.wait_ge(loaded[s].sem, loaded[s].at(name))
                            slots.append(s)
                        for kk in range(2):
                            for half in range(2):
                                mm = pe.matmul(ps[:, 4 + 2 * t + half, :], lhs(kk, t),
                                               ring[:, slots[i], kk * D + half * 512:kk * D + half * 512 + 512],
                                               start=False, stop=(i == 1 and kk == 1))
                        if t == 1:
                            mm.then_inc(used[slots[i]].sem, 1)
                    if t == 0:
                        mm.then_inc(pe_full.add(("t0", tag)), 1)

            def open_acc(name):
                for b in range(4, 8):
                    open_bank(b, name)

            def transposes(tag, src, ready):
                for t in range(TT):
                    ready(t)
                    for j in range(4):
                        if t == 0:
                            open_bank(j, ("T", tag))
                        for kk in range(2):
                            k = 2 * j + kk
                            mm = pe.transpose(ps[:, j, kk * T + t * P:kk * T + t * P + P],
                                              src[:, t, k * P:k * P + P], ident[:])
                mm.then_inc(pe_full.add(("T", tag)), 1)

            def all_copied(tag):
                for j in range(4):
                    pe.wait_ge(emptied[j].sem, emptied[j].at(("T", tag), 1))

            def after_ln(tag):
                def ready(t):
                    pe.wait_ge(dve_done.sem, dve_done.at(("hn", tag, t)))
                transposes(tag, hn, ready)
                all_copied(tag)

            def ffn(tag):
                xh, xl = (wr(at, 2048).rearrange("p (k t) -> p k t", k=DT) for at in (HTH, HTL))

                def gate_up(c, i=None):
                    for what, bank, at in (("gate", 2 * (c % 2), GH_), ("up", 2 * (c % 2) + 1, UH_)):
                        name = key(tag, what, c)
                        open_bank(bank, name)
                        pe.wait_ge(lo_done.sem, chunk_event(lo_done, tag, what, c, i))
                        s = slot_of[name]
                        for pt in range(2):
                            for k in range(DT):
                                o = k * CH + pt * P
                                high, low = wr(at + o, P), ring_halves[s][:, o:o + P]
                                for n, (wt, x) in enumerate(((high, xh), (high, xl), (low, xh))):
                                    mm = pe.matmul(ps[:, bank, pt * T:pt * T + T], wt, x[:, k, :],
                                                   start=(k == 0 and n == 0), stop=(k == DT - 1 and n == 2))
                        mm.then_inc(used[s].sem, 1)

                def products(c, t, kk, s, at, is_first=False, is_last=False):
                    o = kk * T + t * P
                    high = wr(HDH + 512 * (c % 2) + o, P)
                    low = wr(HDL + 512 * (c % 2) + o, P)
                    for half in range(2):
                        o = kk * D + half * 512
                        wh, wlow = wr(at + o, 512), ring_halves[s][:, o:o + 512]
                        for n, (x, wt) in enumerate(((high, wh), (low, wh), (high, wlow))):
                            mm = pe.matmul(ps[:, 4 + 2 * t + half, :], x, wt,
                                           start=(is_first and n == 0), stop=(is_last and n == 2))
                    return mm

                def down(c, i=None):
                    pe.wait_ge(lo_done.sem, chunk_event(lo_done, tag, "down", c, i))
                    s = slot_of[key(tag, "down", c)]
                    for kk in range(2):
                        for t in range(TT):
                            mm = products(c, t, kk, s, DH_, c == 0 and kk == 0)
                    mm.then_inc(used[s].sem, 1)

                by_columns(key(tag, "gate", 0), 0, hT)
                by_columns(key(tag, "up", 0), 1, hT)
                pe.wait_ge(dve_done.sem, dve_done.at(("low", tag)))
                gate_up(1)
                open_acc((tag, "acc"))
                down(0)
                with counted(book, pe, "c" + tag, 2, emptied + [pe_full]) as i:
                    for c in range(2, 6):
                        gate_up(c, i)
                        down(c - 1, i)
                gate_up(10)
                for t in range(TT):
                    for c, name, at in ((9, key(tag, "down", 5), DH_), (10, key(tag, "down", 10), GH_)):
                        if t == 0:
                            pe.wait_ge(lo_done.sem, chunk_event(lo_done, tag, "down", c))
                            if c == 10:
                                pe.wait_ge(dve_done.sem, dve_done.at(("hidden", tag)))
                        s = slot_of[name]
                        for kk in range(2):
                            mm = products(c, t, kk, s, at, is_last=(c == 10 and kk == 1))
                        if t == 1:
                            mm.then_inc(used[s].sem, 1)
                    if t == 0:
                        mm.then_inc(pe_full.add(("t0", NORM_OF[tag])), 1)

            def level(tag, lv):
                if lv == 0:
                    kk, qq = w(K, 1024), w(Q, 1024)
                else:
                    kk, qq = fk, fq
                    pe.wait_ge(dve_done.sem, dve_done.at(("F", tag, lv)))
                if lv == 8:
                    open_bank(6, ("A", tag, lv, 0))
                    for hd in range(HEADS):
                        mm = pe.matmul(ps[:, 6, hd * P:hd * P + P], kk[:, hd * T:hd * T + P],
                                       qq[:, hd * T + P:hd * T + T], start=True, stop=True)
                    mm.then_inc(pe_full.add(("A", tag, lv, 0)), 1)
                    return
                for t in range(TT):
                    b = (6 if lv % 2 == 0 else 2) + t
                    open_bank(b, ("A", tag, lv, t))
                    for hd in range(HEADS):
                        o = hd * T + t * P
                        mm = pe.matmul(ps[:, b, hd * P:hd * P + P], kk[:, o:o + P], qq[:, o:o + P],
                                       start=True, stop=True)
                    mm.then_inc(pe_full.add(("A", tag, lv, t)), 1)

            def outputs(tag, units, vals):
                per = units // HEADS
                pe.wait_ge(dve_done.sem, dve_done.at(("attn", tag)))
                for j in range(units // 2):
                    b = obank(tag, j)
                    open_bank(b, ("O", tag, j))
                    for uu in range(2):
                        u = 2 * j + uu
                        hd = u // per
                        pe.matmul(ps[:, b, uu * T:uu * T + P], vals[:, 0, u * P:u * P + P],
                                  attn[:, 0, hd, :], start=True, stop=True)
                        pe.matmul(ps[:, b, uu * T + P:uu * T + T], vals[:, 0, u * P:u * P + P],
                                  cross[:, hd, :], start=True, stop=False)
                        mm = pe.matmul(ps[:, b, uu * T + P:uu * T + T], vals[:, 1, u * P:u * P + P],
                                       attn[:, 1, hd, :], start=False, stop=True)
                    mm.then_inc(pe_full.add(("O", tag, j)), 1)

            pe.wait_ge(first.sem, 16 * 6)
            transposes("x", h, lambda t: None)
            transposes("mem", w(KT, 2048, "p (t n) -> p t n", t=TT), lambda t: None)
            all_copied("mem")
            pe.wait_ge(prm.sem, prm.at("rows"))
            open_bank(0, "params")
            for b, n in enumerate((128, 102, 32)):
                mm = pe.transpose(ps[:, 0, b * P:b * P + n], work[0:n, Y + b * P:Y + b * P + P], ident[0:n, 0:n])
            mm.then_inc(pe_full.add("params"), 1)

            with counted(book, pe, "L", LAYERS, emptied + [pe_full]) as L:
                ffn("f1")
                after_ln(0)
                by_columns("rf0", 0, hT)
                by_columns("rf1", 1, hT)
                by_columns("rq0", 2, hT)
                by_columns("rq1", 3, hT)
                by_columns("cc", 0, hT)
                pe.wait_ge(emptied[2].sem, emptied[2].at("rq0", 1))
                pe.wait_ge(emptied[3].sem, emptied[3].at("rq1", 1))
                pe.wait_ge(dve_done.sem, dve_done.at(("k", "r")))
                level("r", 0)
                by_columns("ch", 1, hT)
                level("r", 1)
                by_columns("cb", 0, hT)
                level("r", 2)
                by_columns("pu", 1, hT)
                level("r", 3)
                for t in range(TT):
                    open_bank(4 + t, "ri")
                for j in range(2):
                    s = arrived(f"ri{j}")
                    for t in range(TT):
                        for k in range(4):
                            mm = pe.matmul(ps[:, 4 + t, :], hT[:, 4 * j + k, t * P:t * P + P],
                                           ring[:, s, k * 512:k * 512 + 512],
                                           start=(j == 0 and k == 0), stop=(j == 1 and k == 3))
                    mm.then_inc(used[s].sem, 1)
                level("r", 4)
                for j in range(4):
                    by_columns(f"ck{j}", j % 2, memT)
                    level("r", 5 + j)
                open_bank(2, "pool")
                pe.wait_ge(pool_done.sem, pool_done.at("pooled"))
                pe.wait_ge(prm.sem, prm.at(("wpool", 3)))
                pm = w(PM, 512)
                for kt in range(2):
                    mm = pe.matmul(ps[:, 2, kt * T:kt * T + T], wpool[:, kt, :], pm[:, kt * T:kt * T + T],
                                   start=True, stop=True)
                mm.then_inc(pe_full.add("pool"), 1)
                open_acc("cv")
                for j in range(4):
                    by_rows(f"cv{j}", lambda kk, t: memT[:, 2 * j + kk, t * P:t * P + P], j == 0, j == 3)
                for t in range(TT):
                    pe.wait_ge(emptied[4 + t].sem, emptied[4 + t].at("ri", 1))
                outputs("r", 4, w(V, 1024, "p (t n) -> p t n", t=TT))
                by_columns("rg0", 0, hT)
                by_columns("rg1", 1, hT)
                for j in range(2):
                    open_bank(j, ("ms", "r", j))
                    pe.wait_ge(act_done.sem, act_done.at(("sq", "r", j)))
                    pe.matmul(ps[:, j, :], ones[:], work[:, PR + 512 * j:PR + 512 * j + 512], start=True, stop=True)\
                        .then_inc(pe_full.add(("ms", "r", j)), 1)
                open_acc("wo")
                for j, k0 in enumerate((0, 6)):
                    if j == 0:
                        pe.wait_ge(pool_done.sem, pool_done.at("conv"))
                    if j == 1:
                        pe.wait_ge(emptied[2].sem, emptied[2].at("pool", 1))
                    by_rows(f"wo{j}", lambda kk, t: yT[:, k0 + kk, t * P:t * P + P], j == 0, False)
                last_rows(1, [(f"wo{j}", lambda kk, t, k0=k0: yT[:, k0 + kk, t * P:t * P + P],
                               lambda j=j: pe.wait_ge(dve_done.sem, dve_done.at(("y", "r", j - 2))))
                              for j, k0 in ((2, 2), (3, 4))])
                after_ln(1)

                def scores(hd):
                    pe.wait_ge(emptied[2 + hd % 2].sem, emptied[2 + hd % 2].at(f"cq{hd}", 1))
                    b = hd % 2
                    open_bank(b, ("sc", hd))
                    for t in range(TT):
                        for kk in range(2):
                            mm = pe.matmul(ps[:, b, t * T:t * T + T],
                                           work[:, Q + (2 * hd + kk) * T + t * P:Q + (2 * hd + kk) * T + t * P + P],
                                           keyT[:, 2 * hd + kk, :], start=(kk == 0), stop=(kk == 1))
                    mm.then_inc(pe_full.add(("sc", hd)), 1)

                def weighted(hd):
                    pe.wait_ge(dve_done.sem, dve_done.at(("p", hd)))
                    open_bank(2, ("pT", hd))
                    prob = w(FQ + 512 * (hd % 2), 512, "p (t m) -> p t m", t=TT)
                    for t in range(TT):
                        for mt in range(2):
                            mm = pe.transpose(ps[:, 2, mt * T + t * P:mt * T + t * P + P],
                                              prob[:, t, mt * P:mt * P + P], ident[:])
                    mm.then_inc(pe_full.add(("pT", hd)), 1)
                    pe.wait_ge(emptied[2].sem, emptied[2].at(("pT", hd), 1))
                    open_bank(3, ("co", hd))
                    pT = w(FK + 512 * (hd % 2), 512, "p (m t) -> p m t", m=2)
                    for dd in range(2):
                        for mt in range(2):
                            c0 = hd * 256 + dd * P
                            mm = pe.matmul(ps[:, 3, dd * T:dd * T + T], valm[:, mt, c0:c0 + P], pT[:, mt, :],
                                           start=(mt == 0), stop=(mt == 1))
                    mm.then_inc(pe_full.add(("co", hd)), 1)

                by_columns("cq0", 2, hT)
                by_columns("cq1", 3, hT)
                scores(0)
                by_columns("cq2", 2, hT)
                scores(1)
                by_columns("cq3", 3, hT)
                weighted(0)
                scores(2)
                weighted(1)
                scores(3)
                weighted(2)
                weighted(3)
                open_acc("co")
                mixed = w(PR, 2048, "p (g t) -> p g t", g=8)
                for j in range(2):
                    pe.wait_ge(emptied[3].sem, emptied[3].at(("co", j), 1))
                    by_rows(f"co{j}", lambda kk, t: mixed[:, 2 * j + kk, t * P:t * P + P], j == 0, False)
                last_rows(2, [(f"co{j}", lambda kk, t, j=j: mixed[:, 2 * j + kk, t * P:t * P + P],
                               lambda j=j: pe.wait_ge(emptied[3].sem, emptied[3].at(("co", j), 1)))
                              for j in (2, 3)])
                after_ln(2)
                ffn("f2")
                after_ln(3)

            for j in range(4):
                by_columns(f"xa{j}", j, hT)
            for j in range(2):
                by_columns(f"q{j}", j, hT)
            for j in range(2):
                by_columns(f"k{j}", 2 + j, hT)
            open_bank(0, "glr")
            s = arrived("glr")
            for k in range(DT):
                mm = pe.matmul(ps[0:16, 0, 0:T], ring[:, s, k * 16:k * 16 + 16], hT[:, k, :],
                               start=(k == 0), stop=(k == DT - 1))
            mm.then_inc(used[s].sem, 1)
            open_acc("v")
            for j in range(4):
                by_rows(f"v{j}", lambda kk, t: hT[:, 2 * j + kk, t * P:t * P + P], j == 0, j == 3)
            pe.wait_ge(emptied[0].sem, emptied[0].at("glr", 1))
            s = arrived("glg")
            for j in range(2):
                open_bank(j, ("zg", j))
                for kk in range(2):
                    c0 = (2 * j + kk) * P
                    mm = pe.matmul(ps[:, j, kk * T:kk * T + T], ring[0:16, s, c0:c0 + P], work[0:16, FQ:FQ + T],
                                   start=True, stop=True)
                if j == 0:
                    mm.then_inc(pe_full.add(("zg", 0)), 1)
            mm.then_inc(used[s].sem, 1)
            by_columns("go0", 0, hT)
            by_columns("go1", 1, hT)
            pe.wait_ge(dve_done.sem, dve_done.at("xc"))
            for which in ("r", "i"):
                s = arrived("lru" + which)
                for j in range(4):
                    b = 2 + j % 2
                    open_bank(b, ("lru", which, j))
                    for kk in range(2):
                        g = 2 * j + kk
                        mm = pe.matmul(ps[:, b, kk * T:kk * T + T], ring[:, s, g * P:g * P + P],
                                       work[:, XC + g * T:XC + g * T + T], start=True, stop=True)
                    if j < 3:
                        mm.then_inc(pe_full.add(("lru", which, j)), 1)
                mm.then_inc(used[s].sem, 1)
            by_columns("go2", 0, hT)
            by_columns("go3", 1, hT)
            for j in range(2):
                pe.wait_ge(emptied[j].sem, emptied[j].at(f"q{j}", 1))
                pe.wait_ge(emptied[2 + j].sem, emptied[2 + j].at(f"k{j}", 1))
            level("g", 0)
            for j in range(4):
                by_columns(f"mb{j}", j % 2, hT)
                level("g", 1 + j)
            for j in range(4):
                by_columns(f"ga{j}", j % 2, hT)
                level("g", 5 + j)
            for b in range(4, 8):
                pe.wait_ge(emptied[b].sem, emptied[b].at("v", 1))
            outputs("g", 8, w(V, 2048, "p (t n) -> p t n", t=TT))
            by_columns("ma0", 0, hT)
            by_columns("ma1", 1, hT)
            for j in range(2):
                open_bank(j, ("ms", "g", j))
                for hh in range(2):
                    pe.wait_ge(act_done.sem, act_done.at(("sq", "g", 2 * j + hh)))
                    for uu in range(2):
                        u = 2 * (2 * j + hh) + uu
                        mm = pe.matmul(ps[:, j, hh * T:hh * T + T], ones[:], work[:, PR + u * T:PR + u * T + T],
                                       start=(uu == 0), stop=(uu == 1))
                mm.then_inc(pe_full.add(("ms", "g", j)), 1)
            by_columns("ma2", 0, hT)
            by_columns("ma3", 1, hT)
            open_acc("w2o")
            for j in range(2):
                pe.wait_ge(dve_done.sem, dve_done.at(("y", "g", j)))
                by_rows(f"w2o{j}", lambda kk, t: yT[:, 2 * j + kk, t * P:t * P + P], j == 0, False)
            last_rows("A", [(f"w2o{j}", lambda kk, t, j=j: yT[:, 2 * j + kk, t * P:t * P + P],
                             lambda j=j: pe.wait_ge(dve_done.sem, dve_done.at(("y", "g", j)))) for j in (2, 3)])
            after_ln("A")

            open_bank(0, "router")
            s = arrived("router")
            for t in range(TT):
                pe.matmul(ps[:, 0, t * 32:t * 32 + 32], ones[0:1, :], brout[0:1, :], start=True, stop=False)
                for k in range(DT):
                    mm = pe.matmul(ps[:, 0, t * 32:t * 32 + 32], hT[:, k, t * P:t * P + P],
                                   ring[:, s, k * 32:k * 32 + 32], start=False, stop=(k == DT - 1))
            mm.then_inc(used[s].sem, 1)
            open_bank(1, "bup")
            s = arrived("bup")
            for b in range(4):
                mm = pe.transpose(ps[:, 1, b * P:b * P + P], ring[:, s, b * P:b * P + P], ident[:])
            mm.then_inc(used[s].sem, 1)
            open_bank(2, "gT")
            pe.wait_ge(dve_done.sem, dve_done.at("gates"))
            for t in range(TT):
                mm = pe.transpose(ps[0:32, 2, t * P:t * P + P], work[:, GATES + t * 32:GATES + t * 32 + 32], ident[:])
            mm.then_inc(pe_full.add("gT"), 1)
            pe.wait_ge(emptied[2].sem, emptied[2].at("gT", 1))
            open_acc("bd")
            s = arrived("bdown")
            for t in range(TT):
                for half in range(2):
                    mm = pe.matmul(ps[:, 4 + 2 * t + half, :], work[0:32, GT + t * P:GT + t * P + P],
                                   ring[0:32, s, half * 512:half * 512 + 512], start=True, stop=True)
            mm.then_inc(used[s].sem, 1)

            open_bank(0, "pos")
            s = arrived("before")
            chosen = [work[:, CHOSEN + 32 * t:CHOSEN + 32 * t + 32] for t in range(TT)]
            before = ring[:, s, 0:P]
            for o, terms in ((0, [(before, chosen[0])]), (32, [(ones[:], chosen[0]), (before, chosen[1])]),
                             (64, [(ones[:], chosen[0]), (ones[:], chosen[1])])):
                for i, (lhs, rhs) in enumerate(terms):
                    mm = pe.matmul(ps[:, 0, o:o + 32], lhs, rhs, start=(i == 0), stop=(i == len(terms) - 1))
            mm.then_inc(pe_full.add("pos"), 1)

            def gather(name):
                open_bank(2, name)
                for k in range(DT):
                    for t in range(TT):
                        mm = pe.matmul(ps[:, 2, k * CAP:k * CAP + CAP], h[:, t, k * P:k * P + P],
                                       work[:, GS + t * CAP:GS + t * CAP + CAP], start=(t == 0), stop=(t == TT - 1))
                mm.then_inc(pe_full.add(name), 1)

            def combine(name):
                for t in range(TT):
                    for half in range(2):
                        lo = half * CAP
                        mm = pe.matmul(ps[:, 4 + 2 * t + half, :], work[lo:lo + CAP, GGT + t * P:GGT + t * P + P],
                                       work[lo:lo + CAP, YS:YS + 512], start=False, stop=False,
                                       skip_group_check=True)
                mm.then_inc(pe_full.add(name), 1)

            def few():
                pe.wait_ge(h_ready.sem, h_ready.at(("h", "A")))
                pe.wait_ge(sel_ready.sem, sel_ready.at("sel0"))
                gather("xg0")
                with counted(book, pe, "few", EXPERTS, emptied + [pe_full], "e") as e:
                    def gate_up(x):
                        open_bank(x, ("gu", x))
                        if x == 0:
                            pe.wait_ge(emptied[2].sem, emptied[2].at("xg"))
                        for j in (2 * x, 2 * x + 1):
                            pair = [arrived(("moe", what, j)) for what in "gu"]
                            for k in range(DT):
                                for lo, s in zip((0, CAP), pair):
                                    mm = pe.matmul(ps[lo:lo + CAP, x, j % 2 * CH:j % 2 * CH + CH],
                                                   work[:, XG + k * CAP:XG + k * CAP + CAP],
                                                   ring[:, s, k * CH:k * CH + CH],
                                                   start=(k == 0), stop=(k == DT - 1))
                                    if k == DT - 1:
                                        mm.then_inc(used[s].sem, 1)

                    def turned(x):
                        pe.wait_ge(emptied[x].sem, emptied[x].at(("gu", x), 1))
                        emptied[x].add(("gut", x))
                        for f in range(4):
                            mm = pe.transpose(ps[:, x, f * P:f * P + P],
                                              work[:, GUT + 512 * x + f * P:GUT + 512 * x + f * P + P], ident[:])
                        mm.then_inc(pe_full.add(("gut", x)), 1)

                    gate_up(0)
                    gate_up(1)
                    turned(0)
                    pe.wait_ge(sel_ready.sem, sel_ready.at("sel"))
                    gather("xg")
                    turned(1)
                    combine("back")
                    open_bank(2, "GT")
                    for t in range(TT):
                        mm = pe.transpose(ps[:, 2, t * P:t * P + P], work[:, GG + t * P:GG + t * P + P], ident[:])
                    mm.then_inc(pe_full.add("GT"), 1)
                    open_bank(3, "y")
                    for j in range(4):
                        if j % 2 == 0:
                            pe.wait_ge(dve_done.sem, dve_done.at(("few", j // 2)))
                        s = arrived(("moe", "d", j))
                        for kk in range(2):
                            f = 2 * j + kk
                            for half in range(2):
                                mm = pe.matmul(ps[half * CAP:half * CAP + CAP, 3, :],
                                               work[:, ACTS + f * CAP:ACTS + f * CAP + CAP],
                                               ring[:, s, kk * D + half * 512:kk * D + half * 512 + 512],
                                               start=(f == 0), stop=(f == DT - 1))
                        mm.then_inc(used[s].sem, 1)
                pe.wait_ge(emptied[3].sem, emptied[3].at("y", 1, few=EXPERTS - 1))
                combine("last")

            def many():
                with counted(book, pe, "many", EXPERTS, emptied + [pe_full], "e") as e:
                    def gate_up(j):
                        by_columns(("moe", "g", j), 2 * (j % 2), hT, ("all", "g", j))
                        by_columns(("moe", "u", j), 2 * (j % 2) + 1, hT, ("all", "u", j))

                    def down(j):
                        pe.wait_ge(dve_done.sem, dve_done.at(("act", j)))
                        by_rows(("moe", "d", j), lambda kk, t: work[:, ACTT + (2 * j + kk) * T + t * P:ACTT + (2 * j + kk) * T + t * P + P],
                                j == 0, j == 3)

                    gate_up(0)
                    gate_up(1)
                    open_acc("moe")
                    down(0)
                    gate_up(2)
                    down(1)
                    gate_up(3)
                    down(2)
                    down(3)

            pe.wait_ge(dve_done.sem, dve_done.at("most"))
            lines = emptied + [pe_full]
            fork = Fork(book, pe, "experts", lines)
            n = pe.value_load(most[0:1, 0:1])
            with pe.If(n < CAP + 1):
                few()
                fork.end("few", [1] * 8 + [0])
            with pe.Else():
                many()
                fork.end("many", [1] * 8 + [0])
            fork.join()

            open_bank(0, "ptok")
            s = arrived("ptok")
            for t in range(TT):
                for kt in range(2):
                    mm = pe.transpose(ps[:, 0, kt * T + t * P:kt * T + t * P + P],
                                      ring[:, s, t * 256 + kt * P:t * 256 + kt * P + P], ident[:])
            mm.then_inc(used[s].sem, 1)
            pe.wait_ge(emptied[0].sem, emptied[0].at("ptok", 1))
            after_ln("B")
            s = arrived("bpg")
            open_acc("pg")
            for t in range(TT):
                for half in range(2):
                    mm = pe.matmul(ps[:, 4 + 2 * t + half, :], ones[0:1, :], ring[0:1, s, half * 512:half * 512 + 512],
                                   start=True, stop=False)
            mm.then_inc(used[s].sem, 1)
            for j in range(4):
                by_rows(f"pg{j}", lambda kk, t: hT[:, 2 * j + kk, t * P:t * P + P], False, j == 3)
            s = arrived("wple")
            for t in range(TT):
                for half in range(2):
                    b = 2 * t + half
                    open_bank(b, "ple")
                    for kk in range(2):
                        mm = pe.matmul(ps[:, b, :], work[:, FQ + kk * T + t * P:FQ + kk * T + t * P + P],
                                       ring[:, s, kk * D + half * 512:kk * D + half * 512 + 512],
                                       start=(kk == 0), stop=(kk == 1))
            mm.then_inc(used[s].sem, 1)

        @block.scalar
        def _(act):
            def done(ins, name):
                ins.then_inc(act_done.add(name), 1)

            def mine(name):
                act.wait_ge(act_done.sem, act_done.at(name))

            def copy_out(name, bank, dst, full):
                full()
                nc.scalar.copy(dst, ps[:, bank, :]).then_inc(emptied[bank].sem, 1)

            def pe_group(name):
                act.wait_ge(pe_full.sem, pe_full.at(name))

            def row(name, b, at):
                src = a[name]
                flat = {1: "a -> a", 2: "a n -> (a n)", 3: "a b n -> (a b n)"}[len(src.shape)]
                v = src.rearrange(flat).rearrange("(r n) -> r n", n=P)
                act.dma_start(work[at:at + v.shape[0], Y + b * P:Y + b * P + P], v)\
                    .then_inc(prm.add("rows" if name == "ln2_b_2" else ("row", name)), 16)

            for b, group in enumerate((COLS1, COLS2, COLS3)):
                at = 0
                for nm, n in group:
                    row(nm, b, at)
                    at += n

            def evac_T(tag, gname=None, i=None, dst=None):
                pe_group(("T", tag))
                for k in range(4):
                    bank = ps[:, k // 2, (k % 2) * T:(k % 2) * T + T]
                    if gname is None:
                        ins = nc.scalar.copy(dst[:, k, :], bank)
                    else:
                        ins = nc.scalar.activation(dst[:, k, :], bank, ACT.Identity,
                                                   bias=col(gname[1], i + k), scale=col(gname[0], i + k))
                    if k % 2:
                        ins.then_inc(emptied[k // 2].sem, 1)

            def ln(tag, gname, i):
                for t in range(TT):
                    act.wait_ge(dve_done.sem, dve_done.at(("var", tag, t)))
                    done(nc.scalar.activation(rstd[:, t:t + 1], mv[:, t, 1:2], ACT.Sqrt, bias=epsc[:, 0:1]),
                         ("std", tag, t))
                evac_T(tag, gname, i, hT)

            def ffn(tag):
                def high(what, c, at, again="", plus=0, **iters):
                    name = key(tag, what, c)
                    s = slot_of[name]
                    act.wait_ge(loaded[s].sem, loaded[s].at(name, plus, **iters))
                    nc.scalar.copy(wr(at, SLOT), ring[:, s, :])\
                        .then_inc(hi_done.add((tag, what, c) + ((again,) if again else ())), 1)

                def silu(c):
                    slot_used(act, key(tag, "gate", c))
                    nc.scalar.activation(w(FQ + 512 * (c % 2), 512), ps[:, 2 * (c % 2), :], ACT.Silu)\
                        .then_inc(emptied[2 * (c % 2)].sem, 1)

                def hidden(c):
                    b = 2 * (c % 2) + 1
                    act.wait_ge(emptied[b].sem, emptied[b].at(key(tag, "up", c), 1))
                    done(nc.scalar.copy(wr(HDH + 512 * (c % 2), 512), w(FK + 512 * (c % 2), 512)), ("hid", tag, c))

                for b, (what, c) in enumerate((("gate", 0), ("up", 0), ("gate", 1), ("up", 1))):
                    act.wait_ge(emptied[b].sem, emptied[b].at(key(tag, what, c)))
                done(nc.scalar.copy(wr(HTH, 2048), hT[:].rearrange("p k t -> p (k t)")), ("high", tag))
                high("gate", 1, GH_)
                silu(0)
                hidden(0)
                high("up", 1, UH_)
                high("down", 0, DH_)
                silu(1)
                high("gate", 2, GH_, "first", **{"c" + tag: 0})
                hidden(1)
                high("up", 2, UH_, "first", **{"c" + tag: 0})
                with counted(book, act, "c" + tag, 2, [act_done, hi_done]) as i:
                    for c in range(2, 6):
                        if c < 4:
                            slot_used(act, key(tag, "down", c - 2), i)
                        else:
                            slot_used(act, key(tag, "down", c - 2))
                        high("down", c - 1, DH_, *(("loop", i) if c == 2 else ()))
                        silu(c)
                        if c < 5:
                            high("gate", c + 1, GH_)
                        else:
                            high("gate", 2, GH_, "loop", 1)
                        hidden(c)
                        if c < 5:
                            high("up", c + 1, UH_)
                        else:
                            high("up", 2, UH_, "loop", 1)
                last = {"c" + tag: 1}
                slot_used(act, key(tag, "down", 4), **last)
                high("down", 5, DH_, "last", **last)
                silu(10)
                high("down", 10, GH_)
                hidden(10)

            def squares(tag, units):
                for j in range(units // 2):
                    pe_group(("O", tag, j))
                    done(nc.scalar.activation(work[:, PR + 512 * j:PR + 512 * j + 512], ps[:, obank(tag, j), :],
                                              ACT.Square), ("sq", tag, j))

            def roots(tag, n, eps):
                for j in range(2):
                    pe_group(("ms", tag, j))
                    nc.scalar.activation(work[:, Q + 512 * j:Q + 512 * j + 512], ps[:, j, :], ACT.Sqrt,
                                         bias=epsc[:, eps:eps + 1], scale=1.0 / n).then_inc(emptied[j].sem, 1)

            evac_T("x", dst=hT)
            evac_T("mem", dst=memT)
            pe_group("params")
            flat = cols[:].rearrange("p b n -> p (b n)")
            nc.scalar.copy(flat[:, 0:230], ps[:, 0, 0:230])
            nc.scalar.copy(flat[:, 256:288], ps[:, 0, 256:288]).then_inc(emptied[0].sem, 1)
            act.wait_ge(emptied[0].sem, emptied[0].at("params", 1))
            done(nc.scalar.activation(small[:, 0:8], col("lru_lambda_2", 0, 8), ACT.Abs), "abs")
            mine("abs")
            done(nc.scalar.activation(small[:, 8:16], small[:, 0:8], ACT.Exp, scale=-1.0), "lexp")
            mine("lexp")
            act.wait_ge(dve_done.sem, dve_done.at("consts0"))
            done(nc.scalar.activation(small[:, 16:24], small[:, 8:16], ACT.Ln, bias=epsc[:, 2:3]), "lln")
            done(nc.scalar.activation(small[:, 32:40], small[:, 24:32], ACT.Exp), "lbexp")

            with counted(book, act, "L", LAYERS, [act_done, hi_done, prm]) as L:
                for g in range(4):
                    lo = 64 * (g % 2)
                    act.dma_start(wpool[lo:lo + 64, g // 2, lo:lo + 64],
                                  a["pool_w"].rearrange("l g c d -> c (l g) d")[:, bass.ds(L * 4 + g, 1), :]
                                  .rearrange("c a d -> c (a d)")).then_inc(prm.add(("wpool", g)), 16)
                ffn("f1")
                ln(0, ("ln_g", "ln_b"), L * 32)
                for j in range(2):
                    slot_used(act, f"rf{j}")
                    nc.scalar.activation(work[:, FQ + 512 * j:FQ + 512 * j + 512], ps[:, j, :], ACT.Sigmoid)\
                        .then_inc(emptied[j].sem, 1)
                for j in range(2):
                    copy_out(None, 2 + j, work[:, Q + 512 * j:Q + 512 * j + 512], lambda: slot_used(act, f"rq{j}"))
                copy_out(None, 0, w(CC, 512), lambda: slot_used(act, "cc"))
                slot_used(act, "cb")
                act.wait_ge(emptied[1].sem, emptied[1].at("ch", 1))
                nc.scalar.copy(w(CC, 512), ps[:, 0, :]).then_inc(emptied[0].sem, 1)
                slot_used(act, "pu")
                nc.scalar.copy(w(PU, 544, "p (g t) -> p g t", g=2)[:, :, 16:272],
                               ps[:, 1, :].rearrange("p (g t) -> p g t", g=2)).then_inc(emptied[1].sem, 1)
                slot_used(act, "ri1")
                for t in range(TT):
                    nc.scalar.copy(work[:, V + 512 * t:V + 512 * t + 512], ps[:, 4 + t, :])\
                        .then_inc(emptied[4 + t].sem, 1)
                for j in range(4):
                    copy_out(None, j % 2, work[:, KT + 512 * j:KT + 512 * j + 512], lambda: slot_used(act, f"ck{j}"))
                pe_group("pool")
                for kt in range(2):
                    ins = nc.scalar.mul(yT[:, 6 + kt, :], ps[:, 2, kt * T:kt * T + T], col("pool_scale", L * 2 + kt))
                ins.then_inc(emptied[2].sem, 1)
                slot_used(act, "cv3")
                for b in range(4, 8):
                    t, half = (b - 4) // 2, b % 2
                    nc.scalar.copy(valm[:, t, half * 512:half * 512 + 512], ps[:, b, :]).then_inc(emptied[b].sem, 1)
                squares("r", 4)
                for j in range(2):
                    slot_used(act, f"rg{j}")
                    nc.scalar.activation(work[:, Y + 512 + 512 * j:Y + 1024 + 512 * j], ps[:, j, :], ACT.Sigmoid)\
                        .then_inc(emptied[j].sem, 1)
                roots("r", 128, 1)
                ln(1, ("ln_g", "ln_b"), L * 32 + 8)

                def q_copy(j):
                    copy_out(None, 2 + j % 2, work[:, Q + 512 * j:Q + 512 * j + 512], lambda: slot_used(act, f"cq{j}"))

                def expo(hd):
                    b = hd % 2
                    act.wait_ge(dve_done.sem, dve_done.at(("nm", hd)))
                    for t in range(TT):
                        ins = nc.scalar.activation(work[:, FQ + 512 * b + t * T:FQ + 512 * b + t * T + T],
                                                   ps[:, b, t * T:t * T + T], ACT.Exp, bias=smax[:, hd, t:t + 1],
                                                   scale=1.0 / 16, accum_out=ssum[:, hd, t:t + 1])
                        if t == 1:
                            ins.then_inc(emptied[b].sem, 1)

                def p_copy(hd):
                    copy_out(None, 2, w(FK + 512 * (hd % 2), 512), lambda: pe_group(("pT", hd)))

                q_copy(0)
                q_copy(1)
                expo(0)
                q_copy(2)
                expo(1)
                q_copy(3)
                p_copy(0)
                expo(2)
                p_copy(1)
                expo(3)
                p_copy(2)
                p_copy(3)
                ln(2, ("ln_g", "ln_b"), L * 32 + 16)
                ffn("f2")
                ln(3, ("ln_g", "ln_b"), L * 32 + 24)

            xa = w(XA, 2072, "p (g t) -> p g t", g=8)
            for j in range(4):
                slot_used(act, f"xa{j}")
                nc.scalar.copy(xa[:, 2 * j:2 * j + 2, 3:259], ps[:, j, :].rearrange("p (g t) -> p g t", g=2))\
                    .then_inc(emptied[j].sem, 1)
            for j in range(2):
                slot_used(act, f"q{j}")
                nc.scalar.mul(work[:, Q + 512 * j:Q + 512 * j + 512], ps[:, j, :], float(P) ** -0.5)\
                    .then_inc(emptied[j].sem, 1)
            for j in range(2):
                copy_out(None, 2 + j, work[:, K + 512 * j:K + 512 * j + 512], lambda: slot_used(act, f"k{j}"))
            slot_used(act, "glr")
            nc.scalar.copy(work[0:16, FQ:FQ + T], ps[0:16, 0, 0:T]).then_inc(emptied[0].sem, 1)
            slot_used(act, "v3")
            for b in range(4, 8):
                t, half = (b - 4) // 2, b % 2
                nc.scalar.copy(work[:, V + t * D + half * 512:V + t * D + half * 512 + 512], ps[:, b, :])\
                    .then_inc(emptied[b].sem, 1)
            for hd in range(HEADS):
                if hd == 0:
                    pe_group(("zg", 0))
                if hd == 2:
                    slot_used(act, "glg")
                ins = nc.scalar.activation(pr[:, hd, :], ps[:, hd // 2, (hd % 2) * T:(hd % 2) * T + T], ACT.Abs,
                                           bias=col("gla_b_gate_2", hd))
                done(ins, ("zabs", hd))
            mine(("zabs", 3))
            done(nc.scalar.activation(w(PR, 1024), w(PR, 1024), ACT.Exp, scale=-1.0), "zexp")
            mine("zexp")
            done(nc.scalar.activation(w(PR, 1024), w(PR, 1024), ACT.Ln, bias=epsc[:, 2:3]), "zln")
            act.wait_ge(dve_done.sem, dve_done.at("logsig"))
            done(nc.scalar.activation(w(PR, 1024), w(SU, 1024), ACT.Exp, scale=1.0 / 16), "decay")
            for which, off, bias in (("r", R, "lru_b_r_2"), ("i", IG, "lru_b_i_2")):
                for j in range(4):
                    b = 2 + j % 2
                    if j < 3:
                        pe_group(("lru", which, j))
                    else:
                        slot_used(act, "lru" + which)
                    for kk in range(2):
                        g = 2 * j + kk
                        ins = nc.scalar.activation(work[:, off + g * T:off + g * T + T], ps[:, b, kk * T:kk * T + T],
                                                   ACT.Sigmoid, bias=col(bias, g))
                    ins.then_inc(emptied[b].sem, 1)
            act.wait_ge(emptied[3].sem, emptied[3].at(("lru", "i", 3), 1))
            for g in range(8):
                ins = nc.scalar.activation(work[:, TH + g * T:TH + g * T + T], work[:, R + g * T:R + g * T + T],
                                           ACT.Tanh, scale=sp8[:, 0, g:g + 1])
            done(ins, "tanh")
            mine("tanh")
            for g in range(8):
                ins = nc.scalar.activation(work[:, R + g * T:R + g * T + T], work[:, R + g * T:R + g * T + T],
                                           ACT.Exp, scale=sp8[:, 1, g:g + 1])
            done(ins, "a")
            act.wait_ge(h_ready.sem, h_ready.at(("h", 3), L=LAYERS - 1))
            gob = hn[:].rearrange("p t n -> p (t n)")
            for j in range(4):
                if j == 2:
                    act.wait_ge(dve_done.sem, dve_done.at("ratio"))
                    done(nc.scalar.activation(w(TH, 2048), w(TH, 2048), ACT.Sqrt, scale=2.0), "mult")
                slot_used(act, f"go{j}")
                nc.scalar.activation(gob[:, 512 * j:512 * j + 512], ps[:, j % 2, :], ACT.Silu)\
                    .then_inc(emptied[j % 2].sem, 1)
            for j in range(4):
                slot_used(act, f"mb{j}")
                if j >= 2:
                    act.wait_ge(pool_done.sem, pool_done.at(("mb", j - 2)))
                if j == 0:
                    act.wait_ge(dve_done.sem, dve_done.at("scan"))
                nc.scalar.activation(work[:, TH + 512 * (j % 2):TH + 512 * (j % 2) + 512], ps[:, j % 2, :],
                                     ACT.Sigmoid).then_inc(emptied[j % 2].sem, 1)
            for nm, fn in (("ga", ACT.Gelu_apprx_tanh), ("ma", ACT.Sigmoid)):
                if nm == "ma":
                    squares("g", 8)
                for j in range(4):
                    if (nm, j) == ("ma", 2):
                        roots("g", 256, 0)
                    slot_used(act, f"{nm}{j}")
                    if j >= 2:
                        act.wait_ge(dve_done.sem, dve_done.at((nm, j - 2)))
                    elif nm == "ma":
                        act.wait_ge(dve_done.sem, dve_done.at(("ga", 2 + j)))
                    nc.scalar.activation(work[:, R + 512 * (j % 2):R + 512 * (j % 2) + 512], ps[:, j % 2, :], fn)\
                        .then_inc(emptied[j % 2].sem, 1)
            ln("A", ("ln1_g_2", "ln1_b_2"), 0)

            act.wait_ge(dve_done.sem, dve_done.at("rmax"))
            for t in range(TT):
                ins = nc.scalar.activation(work[:, GATES + t * 32:GATES + t * 32 + 32],
                                           work[:, LOGIT + t * 32:LOGIT + t * 32 + 32], ACT.Exp,
                                           bias=small[:, 40 + t:41 + t])
            done(ins, "rexp")
            slot_used(act, "bup")
            nc.scalar.copy(w(BUP, 512), ps[:, 1, :]).then_inc(emptied[1].sem, 1)
            pe_group("gT")
            nc.scalar.copy(work[0:32, GT:GT + T], ps[0:32, 2, 0:T]).then_inc(emptied[2].sem, 1)

            def few():
                copy_out(None, 2, w(XG, 512), lambda: pe_group("xg0"))
                with counted(book, act, "few", EXPERTS, [act_done], "e") as e:
                    for x in range(2):
                        copy_out(None, x, w(GUT + 512 * x, 512), lambda: slot_used(act, ("moe", "u", 2 * x + 1)))
                    copy_out(None, 2, w(XG, 512), lambda: pe_group("xg"))
                    for x in range(2):
                        act.wait_ge(dve_done.sem, dve_done.at(("gh", x)))
                        done(nc.scalar.activation(w(SG + 256 * x, 256), w(GH + 256 * x, 256), ACT.Sigmoid,
                                                  scale=SIG_ALPHA), ("sig", x))
                    pe_group("GT")
                    nc.scalar.copy(w(GGT, 256), ps[:, 2, 0:256]).then_inc(emptied[2].sem, 1)
                    copy_out(None, 3, w(YS, 512), lambda: slot_used(act, ("moe", "d", 3)))

            def many():
                with counted(book, act, "many", EXPERTS, [act_done], "e") as e:
                    for j in range(4):
                        act.wait_ge(emptied[2 * (j % 2)].sem, emptied[2 * (j % 2)].at(("all", "g", j), 1))
                        done(nc.scalar.activation(work[:, SG + 512 * (j % 2):SG + 512 * (j % 2) + 512],
                                                  work[:, GH + 512 * (j % 2):GH + 512 * (j % 2) + 512],
                                                  ACT.Sigmoid, scale=SIG_ALPHA), ("sg", j))

            act.wait_ge(dve_done.sem, dve_done.at("most"))
            fork = Fork(book, act, "experts", [act_done])
            n = act.value_load(most[0:1, 0:1])
            with act.If(n < CAP + 1):
                few()
                fork.end("few", [0])
            with act.Else():
                many()
                fork.end("many", [0])
            fork.join()
            slot_used(act, "ptok")
            nc.scalar.copy(w(FQ, 512), ps[:, 0, :]).then_inc(emptied[0].sem, 1)
            ln("B", ("ln2_g_2", "ln2_b_2"), 0)
            slot_used(act, "pg3")
            act.wait_ge(h_ready.sem, h_ready.at(("h", "B")))
            for b in range(4, 8):
                t, half = (b - 4) // 2, b % 2
                nc.scalar.activation(hn[:, t, half * 512:half * 512 + 512], ps[:, b, :], ACT.Sigmoid)\
                    .then_inc(emptied[b].sem, 1)
            for t in range(TT):
                act.wait_ge(dve_done.sem, dve_done.at(("out", t)))
                act.dma_start(a["out"].rearrange("a (t p) n -> p (a t) n", p=P)[:, t, :], h[:, t, :])\
                    .then_inc(out_done.add(t), 16)
            act.wait_ge(out_done.sem, 32)

        @block.vector
        def _(dve):
            v = nc.vector
            links = [0]

            def done(ins, name):
                ins.then_inc(dve_done.add(name), 1)

            def link(ins):
                links[0] += 1
                name = ("link", links[0])
                ins.then_inc(dve_done.add(name), 1)
                dve.wait_ge(dve_done.sem, dve_done.at(name))

            def mine(name):
                dve.wait_ge(dve_done.sem, dve_done.at(name))

            def pe_group(name):
                dve.wait_ge(pe_full.sem, pe_full.at(name))

            def bank_empty(b, name, **iters):
                dve.wait_ge(emptied[b].sem, emptied[b].at(name, 1, **iters))

            def evac_T(tag, gname=None, i=None, dst=None):
                pe_group(("T", tag))
                for k in range(4, 8):
                    bank = ps[:, k // 2, (k % 2) * T:(k % 2) * T + T]
                    if gname is None:
                        ins = v.tensor_copy(dst[:, k, :], bank)
                    else:
                        ins = v.tensor_scalar(dst[:, k, :], bank, col(gname[0], i + k), col(gname[1], i + k),
                                              ALU.mult, ALU.add)
                    if k % 2:
                        ins.then_inc(emptied[k // 2].sem, 1)

            def ln(tag, gname, i, alpha, full, banked=True):
                dve.wait_ge(h_ready.sem, h_ready.at(("h", tag), -1))
                for t in range(TT):
                    if banked and t == 0:
                        pe_group(("t0", tag))
                    if banked and t == 1:
                        full()
                    for half in range(2):
                        c = slice(half * 512, half * 512 + 512)
                        src = ps[:, 4 + 2 * t + half, :] if banked else \
                            work[:, MACC + t * D + half * 512:MACC + t * D + half * 512 + 512]
                        ins = v.scalar_tensor_tensor(out=hn[:, t, c], in0=h[:, t, c], scalar=alpha, in1=src,
                                                     op0=ALU.mult, op1=ALU.add)
                        if banked:
                            ins.then_inc(emptied[4 + 2 * t + half].sem, 1)
                        else:
                            done(ins, ("x", tag, t, half))
                    for half in range(2):
                        if banked:
                            bank_empty(4 + 2 * t + half, acc_name(tag))
                        else:
                            mine(("x", tag, t, half))
                        ins = v.bn_stats(stat[:, t, half, :], hn[:, t, half * 512:half * 512 + 512])
                    done(ins, ("stats", tag, t))
                    mine(("stats", tag, t))
                    plain(dve)
                    done(v.bn_aggr(mv[:, t, :], stat[:, t, :, :].rearrange("p a b -> p (a b)")), ("var", tag, t))
                    dve.wait_ge(act_done.sem, act_done.at(("std", tag, t)))
                    link(v.reciprocal(rstd[:, t:t + 1], rstd[:, t:t + 1]))
                    done(v.tensor_scalar(hn[:, t, :], hn[:, t, :], mv[:, t, 0:1], rstd[:, t:t + 1],
                                         ALU.subtract, ALU.mult), ("hn", tag, t))
                evac_T(tag, gname, i, hT)

            def acc_name(tag):
                return {0: ("f1", "acc"), 1: "wo", 2: "co", 3: ("f2", "acc"), "A": "w2o"}[tag]

            def ffn(tag):
                def low(what, c, at, again=""):
                    name = (tag, what, c) + ((again,) if again else ())
                    s = slot_of[key(tag, what, c)]
                    dve.wait_ge(hi_done.sem, hi_done.at(name))
                    v.tensor_tensor(ring_halves[s][:], ring[:, s, :], wr(at, SLOT).bitcast(F32), ALU.subtract)\
                        .then_inc(lo_done.add(name), 1)

                def up(c):
                    b = 2 * (c % 2) + 1
                    slot_used(dve, key(tag, "up", c))
                    bank_empty(b - 1, key(tag, "gate", c))
                    hid = w(FK + 512 * (c % 2), 512)
                    v.scalar_tensor_tensor(out=hid, in0=w(FQ + 512 * (c % 2), 512), scalar=0.5,
                                           in1=ps[:, b, :], op0=ALU.mult, op1=ALU.mult).then_inc(emptied[b].sem, 1)
                    dve.wait_ge(act_done.sem, act_done.at(("hid", tag, c)))
                    ins = v.tensor_tensor(wr(HDL + 512 * (c % 2), 512), hid, wr(HDH + 512 * (c % 2), 512).bitcast(F32),
                                          ALU.subtract)
                    if c == 10:
                        done(ins, ("hidden", tag))

                dve.wait_ge(act_done.sem, act_done.at(("high", tag)))
                done(v.tensor_tensor(wr(HTL, 2048), hT[:].rearrange("p k t -> p (k t)"),
                                     wr(HTH, 2048).bitcast(F32), ALU.subtract), ("low", tag))
                low("gate", 1, GH_)
                up(0)
                low("up", 1, UH_)
                low("down", 0, DH_)
                low("gate", 2, GH_, "first")
                up(1)
                low("up", 2, UH_, "first")
                with counted(book, dve, "c" + tag, 2, [dve_done, lo_done]):
                    for c in range(2, 6):
                        low("down", c - 1, DH_, "loop" if c == 2 else "")
                        low(*(("gate", c + 1, GH_) if c < 5 else ("gate", 2, GH_, "loop")))
                        up(c)
                        low(*(("up", c + 1, UH_) if c < 5 else ("up", 2, UH_, "loop")))
                low("down", 5, DH_, "last")
                low("down", 10, GH_)
                up(10)

            def decay_step(tag, lv):
                n = 1 << (lv - 1)

                def halves(off):
                    x = w(off, 1024, "p (b a n) -> p b a n", a=2, n=n)
                    return x[:, :, 0, :], x[:, :, 1, :]

                nb = 1024 // (2 * n)
                (q0, q1), (k0, k1), (p0, p1), (s0, s1) = (halves(o) for o in (Q, K, PR, SU))
                fq1, fk0 = halves(FQ)[1], halves(FK)[0]
                if lv >= 2:
                    pe_group(("A", tag, lv - 1, 1))
                v.tensor_tensor(fq1, q1, p1, ALU.mult)
                done(v.tensor_tensor(fk0, k0, s0, ALU.mult), ("F", tag, lv))
                mine(("F", tag, lv))
                if lv < 8:
                    link(v.tensor_tensor(s0, s0, p1[:, :, n - 1:n].broadcast_to([P, nb, n]), ALU.mult))
                    link(v.tensor_tensor(p1, p1, p0[:, :, n - 1:n].broadcast_to([P, nb, n]), ALU.mult))

            def scores_out(tag, lv):
                for t in range(TT):
                    pe_group(("A", tag, lv, t))
                    b = (6 if lv % 2 == 0 else 2) + t
                    plain(dve)
                    v.copy_predicated(attn[:, t, :, :],
                                      mask[:, lv:lv + 1, :].broadcast_to([P, HEADS, P]),
                                      ps[:, b, :].rearrange("p (h s) -> p h s", h=HEADS)).then_inc(emptied[b].sem, 1)

            def last_scores(tag):
                pe_group(("A", tag, 8, 0))
                v.tensor_copy(w(AX_, 512), ps[:, 6, :]).then_inc(emptied[6].sem, 1)
                dve.wait_ge(emptied[6].sem, emptied[6].at(("A", tag, 8, 0), 1))
                done(v.memset(small[:, 63:64], 0.0), ("attn", tag))

            for ins in (v.memset(ones[:], 1.0), v.memset(epsc[:, 0:1], LN_EPS), v.memset(epsc[:, 1:2], 1e-6),
                        v.memset(epsc[:, 2:3], 1.0), v.memset(wpool[:], 0.0), v.memset(w(AA, 1024), 0.0),
                        v.memset(w(FQ, 2048), 0.0), v.memset(w(UP, 516), 0.0), v.memset(w(PU, 544), 0.0)):
                pass
            done(ins, "zeros")
            dve.wait_ge(first.sem, 16 * 6)
            v.tensor_copy(mask[:].rearrange("p l t -> p (l t)"), w(V, 1024))
            evac_T("x", dst=hT)
            evac_T("mem", dst=memT)
            bank_empty(0, "params")
            la, lb_ = col("rec_lb", 0, 4), col("rec_lb", 4, 4)
            link(v.tensor_tensor(small[:, 48:52], la, lb_, ALU.max))
            v.tensor_tensor(small[:, 24:28], la, small[:, 48:52], ALU.subtract)
            done(v.tensor_tensor(small[:, 28:32], lb_, small[:, 48:52], ALU.subtract), "consts0")
            dve.wait_ge(act_done.sem, act_done.at("lbexp"))
            link(v.tensor_tensor(small[:, 52:56], small[:, 32:36], small[:, 36:40], ALU.add))
            link(v.reciprocal(small[:, 52:56], small[:, 52:56]))
            v.tensor_tensor(small[:, 32:36], small[:, 32:36], small[:, 52:56], ALU.mult)
            link(v.tensor_tensor(small[:, 36:40], small[:, 36:40], small[:, 52:56], ALU.mult))
            v.tensor_tensor(lbt[:, 0, 0:4], small[:, 32:36], small[:, 32:36], ALU.subtract)
            link(v.tensor_tensor(small[:, 56:60], small[:, 32:36], small[:, 36:40], ALU.add))
            link(v.tensor_tensor(lbt[:, 0, 4:8], small[:, 56:60], small[:, 32:36], ALU.subtract))
            v.tensor_scalar(lbt[:, 1, :], lbt[:, 0, :], -1.0, 1.0, ALU.mult, ALU.add)
            link(v.tensor_scalar(small[:, 40:48], col("lru_lambda_2", 0, 8), -1.0, 0.0, ALU.mult, ALU.max))
            link(v.tensor_tensor(small[:, 40:48], small[:, 40:48], small[:, 16:24], ALU.add))
            v.tensor_scalar(sp8[:, 0, :], small[:, 40:48], 8.0, None, ALU.mult)
            done(v.tensor_scalar(sp8[:, 1, :], small[:, 40:48], -8.0, None, ALU.mult), "consts")
            mine("consts")

            with counted(book, dve, "L", LAYERS, [dve_done, lo_done]) as L:
                ffn("f1")
                ln(0, ("ln_g", "ln_b"), L * 32, ALPHA, lambda: slot_used(dve, key("f1", "down", 10)))
                for hd in range(HEADS):
                    if hd % 2 == 0:
                        bank_empty(hd // 2, f"rf{hd // 2}")
                    ins = v.tensor_scalar(pr[:, hd, :], work[:, FQ + hd * T:FQ + hd * T + T],
                                          lbt[:, 1, bass.ds(L * 4 + hd, 1)], lbt[:, 0, bass.ds(L * 4 + hd, 1)],
                                          ALU.mult, ALU.add)
                link(ins)
                v.memset(w(SU, 1024), 1.0)
                done(v.tensor_scalar(w(K, 1024), w(PR, 1024), -1.0, 1.0, ALU.mult, ALU.add), ("k", "r"))
                mine(("k", "r"))
                bank_empty(2, "rq0")
                bank_empty(3, "rq1")
                decay_step("r", 1)
                slot_used(dve, "ch")
                bank_empty(0, "cc")
                v.tensor_tensor(w(UP, 516, "p (g t) -> p g t", g=2)[:, :, 2:258],
                                ps[:, 1, :].rearrange("p (g t) -> p g t", g=2),
                                w(CC, 512, "p (g t) -> p g t", g=2), ALU.mult).then_inc(emptied[1].sem, 1)
                scores_out("r", 0)
                for lv in range(2, 9):
                    decay_step("r", lv)
                    scores_out("r", lv - 1)
                last_scores("r")
                for j in range(2):
                    dve.wait_ge(emptied[j].sem, emptied[j].at(("ms", "r", j), 1))
                    link(v.reciprocal(work[:, Q + 512 * j:Q + 512 * j + 512], work[:, Q + 512 * j:Q + 512 * j + 512]))
                    for uu in range(2):
                        u = 2 * j + uu
                        ins = v.scalar_tensor_tensor(out=work[:, FQ + u * T:FQ + u * T + T],
                                                     in0=ps[:, obank("r", j), uu * T:uu * T + T],
                                                     scalar=col("rec_norm_g", L * 4 + u),
                                                     in1=work[:, Q + u * T:Q + u * T + T], op0=ALU.mult, op1=ALU.mult)
                    ins.then_inc(emptied[obank("r", j)].sem, 1)
                    bank_empty(obank("r", j), ("O", "r", j))
                    bank_empty(j, f"rg{j}")
                    done(v.tensor_tensor(work[:, Y + 512 + 512 * j:Y + 1024 + 512 * j],
                                         work[:, Y + 512 + 512 * j:Y + 1024 + 512 * j],
                                         work[:, FQ + 512 * j:FQ + 512 * j + 512], ALU.mult), ("y", "r", j))
                ln(1, ("ln_g", "ln_b"), L * 32 + 8, ALPHA, lambda: slot_used(dve, "wo3"))

                def negmax(hd):
                    b = hd % 2
                    pe_group(("sc", hd))
                    link(v.tensor_reduce(smax[:, hd, :], ps[:, b, :].rearrange("p (t m) -> p t m", t=TT), AX.X, ALU.max))
                    done(v.tensor_scalar(smax[:, hd, :], smax[:, hd, :], -1.0 / 16, None, ALU.mult), ("nm", hd))

                def normalise(hd):
                    bank_empty(hd % 2, ("sc", hd))
                    link(v.reciprocal(ssum[:, hd, :], ssum[:, hd, :]))
                    for t in range(TT):
                        x = work[:, FQ + 512 * (hd % 2) + t * T:FQ + 512 * (hd % 2) + t * T + T]
                        ins = v.tensor_scalar(x, x, ssum[:, hd, t:t + 1], None, ALU.mult)
                    done(ins, ("p", hd))

                def o_copy(hd):
                    pe_group(("co", hd))
                    v.tensor_copy(work[:, PR + 512 * hd:PR + 512 * hd + 512], ps[:, 3, :]).then_inc(emptied[3].sem, 1)

                negmax(0)
                negmax(1)
                normalise(0)
                o_copy(0)
                normalise(1)
                negmax(2)
                o_copy(1)
                normalise(2)
                negmax(3)
                o_copy(2)
                normalise(3)
                o_copy(3)
                ln(2, ("ln_g", "ln_b"), L * 32 + 16, ALPHA, lambda: slot_used(dve, "co3"))
                ffn("f2")
                ln(3, ("ln_g", "ln_b"), L * 32 + 24, ALPHA, lambda: slot_used(dve, key("f2", "down", 10)))

            xa = w(XA, 2072, "p (g t) -> p g t", g=8)
            xc = w(XC, 2048, "p (g t) -> p g t", g=8)
            link(v.memset(xa[:, :, 0:3], 0.0))
            for g in range(8):
                if g % 2 == 0:
                    bank_empty(g // 2, f"xa{g // 2}")
                done(v.tensor_scalar(xc[:, g, :], xa[:, g, 0:T], col("conv_w_2", g), col("conv_b_2", g),
                                     ALU.mult, ALU.add), ("conv", g, 0))
            for k in range(1, 4):
                for g in range(8):
                    mine(("conv", g, k - 1))
                    ins = v.scalar_tensor_tensor(out=xc[:, g, :], in0=xa[:, g, k:k + T], scalar=col("conv_w_2", 8 * k + g),
                                                 in1=xc[:, g, :], op0=ALU.mult, op1=ALU.add)
                    done(ins, "xc" if (k, g) == (3, 7) else ("conv", g, k))
            for hd in range(HEADS):
                dve.wait_ge(act_done.sem, act_done.at(("zabs", hd // 2 * 2 + 1)))
                ins = v.tensor_scalar(su[:, hd, :], ps[:, hd // 2, (hd % 2) * T:(hd % 2) * T + T],
                                      col("gla_b_gate_2", hd), 0.0, ALU.add, ALU.min)
                if hd % 2:
                    ins.then_inc(emptied[hd // 2].sem, 1)
            bank_empty(1, ("zg", 1))
            dve.wait_ge(act_done.sem, act_done.at("zln"))
            done(v.tensor_tensor(w(SU, 1024), w(SU, 1024), w(PR, 1024), ALU.subtract), "logsig")
            dve.wait_ge(act_done.sem, act_done.at("decay"))
            v.memset(w(SU, 1024), 1.0)
            dve.wait_ge(act_done.sem, act_done.at("tanh"))
            link(v.tensor_scalar(w(Y, 2048), w(TH, 2048), 1.0, None, ALU.add))
            link(v.reciprocal(w(Y, 2048), w(Y, 2048)))
            done(v.tensor_tensor(w(TH, 2048), w(TH, 2048), w(Y, 2048), ALU.mult), "ratio")
            dve.wait_ge(act_done.sem, act_done.at("mult"))
            dve.wait_ge(pool_done.sem, pool_done.at("ix"))
            v.memset(w(R, 2048, "p (g t) -> p g t", g=8)[:, :, 0:1], 0.0)
            link(v.tensor_tensor(w(IG, 2048), w(IG, 2048), w(TH, 2048), ALU.mult))
            done(v.tensor_tensor_scan(w(XC, 2048), w(R, 2048), w(IG, 2048), 0.0, ALU.mult, ALU.add), "scan")
            for j in range(2):
                bank_empty(j, f"q{j}")
                bank_empty(2 + j, f"k{j}")
            decay_step("g", 1)
            scores_out("g", 0)
            for lv in range(2, 6):
                decay_step("g", lv)
                scores_out("g", lv - 1)

            def times(nm, j):
                bank_empty(j % 2, f"{nm}{j}")
                x = work[:, XC + 512 * j:XC + 512 * j + 512]
                done(v.tensor_tensor(x, x, work[:, R + 512 * (j % 2):R + 512 * (j % 2) + 512], ALU.mult), (nm, j))

            mine("scan")
            for lv in range(6, 9):
                times("ga", lv - 6)
                decay_step("g", lv)
                scores_out("g", lv - 1)
            times("ga", 3)
            last_scores("g")
            for j in range(2):
                mine(("ga", j))
                times("ma", j)
            dve.wait_ge(pool_done.sem, pool_done.at(("mb", 3)))
            for j in range(2):
                bank_empty(j, ("ms", "g", j))
                link(v.reciprocal(work[:, Q + 512 * j:Q + 512 * j + 512], work[:, Q + 512 * j:Q + 512 * j + 512]))
            for j in range(4):
                for uu in range(2):
                    u = 2 * j + uu
                    ins = v.scalar_tensor_tensor(out=work[:, FQ + u * T:FQ + u * T + T],
                                                 in0=ps[:, obank("g", j), uu * T:uu * T + T],
                                                 scalar=col("gla_norm_g_2", uu), in1=work[:, Q + j * T:Q + j * T + T],
                                                 op0=ALU.mult, op1=ALU.mult)
                ins.then_inc(emptied[obank("g", j)].sem, 1)
                bank_empty(obank("g", j), ("O", "g", j))
                x = work[:, FQ + 512 * j:FQ + 512 * j + 512]
                link(v.tensor_tensor(x, x, hn[:].rearrange("p t n -> p (t n)")[:, 512 * j:512 * j + 512], ALU.mult))
                if j >= 2:
                    mine(("ga", j))
                    times("ma", j)
                mine(("ma", j))
                done(v.tensor_tensor(work[:, Y + 512 * j:Y + 512 * j + 512], x,
                                     work[:, XC + 512 * j:XC + 512 * j + 512], ALU.add), ("y", "g", j))
            ln("A", ("ln1_g_2", "ln1_b_2"), 0, ALPHA2, lambda: slot_used(dve, "w2o3"))

            slot_used(dve, "router")
            v.tensor_copy(work[:, LOGIT:LOGIT + 64], ps[:, 0, 0:64]).then_inc(emptied[0].sem, 1)
            bank_empty(0, "router")
            lg = w(LOGIT, 64, "p (t e) -> p t e", t=TT)
            link(v.tensor_reduce(small[:, 40:42], lg, AX.X, ALU.max))
            done(v.tensor_scalar(small[:, 40:42], small[:, 40:42], -1.0, None, ALU.mult), "rmax")
            s = slot_of["tri"]
            dve.wait_ge(loaded[s].sem, loaded[s].at("tri"))
            for t in range(TT):
                li = lg[:, t:t + 1, :].broadcast_to([P, 32, 32])
                lj = w(LOGIT + 32 * t, 32).rearrange("p (e o) -> p e o", o=1).broadcast_to([P, 32, 32])
                gt = w(CMP, 1024, "p (j i) -> p j i", j=32)
                eq = w(CMP + 1024, 1024, "p (j i) -> p j i", j=32)
                v.tensor_tensor(gt, li, lj, ALU.is_gt)
                link(v.tensor_tensor(eq, li, lj, ALU.is_equal))
                link(v.tensor_tensor(w(CMP + 1024, 1024), w(CMP + 1024, 1024), ring[:, s, 0:1024], ALU.mult))
                link(v.tensor_tensor(w(CMP, 1024), w(CMP, 1024), w(CMP + 1024, 1024), ALU.add))
                link(v.tensor_reduce(work[:, CHOSEN + 32 * t:CHOSEN + 32 * t + 32], gt, AX.X, ALU.add))
            link(v.tensor_scalar(w(CHOSEN, 64), w(CHOSEN, 64), float(TOPK), None, ALU.is_lt))
            v.memset(small[:, 60:61], 0.0).then_inc(used[s].sem, 1)
            dve.wait_ge(act_done.sem, act_done.at("rexp"))
            link(v.tensor_tensor(w(GATES, 64), w(GATES, 64), w(CHOSEN, 64), ALU.mult))
            link(v.tensor_reduce(small[:, 42:44], w(GATES, 64, "p (t e) -> p t e", t=TT), AX.X, ALU.add))
            link(v.reciprocal(small[:, 42:44], small[:, 42:44]))
            for t in range(TT):
                x = work[:, GATES + 32 * t:GATES + 32 * t + 32]
                ins = v.tensor_scalar(x, x, small[:, 42 + t:43 + t], None, ALU.mult)
            done(ins, "gates")
            s = slot_of["before"]
            dve.wait_ge(loaded[s].sem, loaded[s].at("before"))
            v.tensor_copy(w(IOTA, P), ring[:, s, P:2 * P])
            pe_group("pos")
            v.tensor_copy(w(POS, 64), ps[:, 0, 0:64]).then_inc(used[s].sem, 1)
            link(v.tensor_reduce(small[:, 44:45], ps[:, 0, 64:96], AX.X, ALU.max))
            v.tensor_copy(most[:], small[:, 44:45]).then_inc(emptied[0].sem, 1)
            bank_empty(0, "pos")
            done(v.memset(small[:, 62:63], 0.0), "most")
            bank_empty(1, "bup")

            def biases_out():
                for b in range(4, 8):
                    v.tensor_copy(work[:, MACC + 512 * (b - 4):MACC + 512 * (b - 4) + 512], ps[:, b, :])\
                        .then_inc(emptied[b].sem, 1)
                link(v.memset(small[:, 63:64], 0.0))

            def of_expert(i, o):
                return [work[:, bass.ds(i + (at + 32 * o), 1)] if not isinstance(i, int)
                        else work[:, at + 32 * o + i:at + 32 * o + i + 1] for at in (POS, CHOSEN, GATES)]

            def select(i, name):
                for t in range(TT):
                    pos, chosen, _ = of_expert(i, t)
                    ins = v.tensor_scalar(w(GS + t * CAP, CAP), w(IOTA, CAP), pos, chosen, ALU.is_equal, ALU.mult)
                ins.then_inc(sel_ready.add(name), 1)

            def few():
                v.memset(w(GGT, 256), 0.0)
                v.memset(w(YS, 512), 0.0)
                select(0, "sel0")
                with counted(book, dve, "few", EXPERTS, [dve_done, sel_ready], "e") as e:
                    dve.wait_ge(pe_full.sem, pe_full.at(("gut", 0), -1))
                    for t in range(TT):
                        pos, _, gate = of_expert(e, t)
                        v.tensor_scalar(w(GG + t * P, P), w(IOTA, P), pos, gate, ALU.is_equal, ALU.mult)
                    select(e + 1, "sel")
                    for x in range(2):
                        pe_group(("gut", x))
                        bg, bu = (work[:, bass.ds(e * 16 + (BUP + o + 4 * x), 4)].rearrange("p (f o) -> p f o", o=1)
                                  .broadcast_to([P, 4, CAP]) for o in (0, 8))
                        gh, uh = (w(o + 256 * x, 256) for o in (GH, UH))
                        tiles = lambda ap: ap.rearrange("p (f c) -> p f c", f=4)
                        gu = ps[:, x, :].rearrange("p (f c) -> p f c", f=4)
                        link(v.tensor_tensor(tiles(gh), gu[:, :, 0:CAP], bg, ALU.add))
                        done(v.tensor_scalar(gh, gh, LIMIT, None, ALU.min), ("gh", x))
                        v.tensor_tensor(tiles(uh), gu[:, :, CAP:P], bu, ALU.add).then_inc(emptied[x].sem, 1)
                        bank_empty(x, ("gut", x))
                        link(v.tensor_scalar(uh, uh, LIMIT, -LIMIT, ALU.min, ALU.max))
                        link(v.scalar_tensor_tensor(out=uh, in0=uh, scalar=1.0, in1=gh, op0=ALU.add, op1=ALU.mult))
                        dve.wait_ge(act_done.sem, act_done.at(("sig", x)))
                        done(v.tensor_tensor(w(ACTS + 256 * x, 256), uh, w(SG + 256 * x, 256), ALU.mult), ("few", x))
                pe_group("last")
                biases_out()

            def many():
                biases_out()
                with counted(book, dve, "many", EXPERTS, [dve_done], "e") as e:
                    def swish(j):
                        g, b = 2 * (j % 2), 512 * (j % 2)
                        slot_used(dve, ("moe", "g", j))
                        for kk in range(2):
                            ins = v.tensor_scalar(work[:, GH + b + kk * T:GH + b + kk * T + T], ps[:, g, kk * T:kk * T + T],
                                                  work[:, bass.ds(e * 16 + (BUP + 2 * j + kk), 1)], LIMIT, ALU.add, ALU.min)
                        ins.then_inc(emptied[g].sem, 1)
                        slot_used(dve, ("moe", "u", j))
                        for kk in range(2):
                            ins = v.tensor_scalar(work[:, UH + b + kk * T:UH + b + kk * T + T], ps[:, g + 1, kk * T:kk * T + T],
                                                  work[:, bass.ds(e * 16 + (BUP + 8 + 2 * j + kk), 1)], LIMIT, ALU.add, ALU.min)
                        ins.then_inc(emptied[g + 1].sem, 1)
                        bank_empty(g + 1, ("all", "u", j))
                        uh, gh, sg = (work[:, o + b:o + b + 512] for o in (UH, GH, SG))
                        link(v.tensor_scalar(uh, uh, -LIMIT, 1.0, ALU.max, ALU.add))
                        bank_empty(g, ("all", "g", j))
                        link(v.tensor_tensor(uh, uh, gh, ALU.mult))
                        dve.wait_ge(act_done.sem, act_done.at(("sg", j)))
                        done(v.tensor_tensor(work[:, ACTT + 512 * j:ACTT + 512 * j + 512], uh, sg, ALU.mult), ("act", j))

                    for j in range(4):
                        swish(j)
                    slot_used(dve, ("moe", "d", 3))
                    for t in range(TT):
                        for half in range(2):
                            b = 4 + 2 * t + half
                            x = work[:, MACC + t * D + half * 512:MACC + t * D + half * 512 + 512]
                            v.scalar_tensor_tensor(out=x, in0=ps[:, b, :], scalar=work[:, bass.ds(e + (GATES + 32 * t), 1)],
                                                   in1=x, op0=ALU.mult, op1=ALU.add).then_inc(emptied[b].sem, 1)
                    for b in range(4, 8):
                        bank_empty(b, "moe")

            fork = Fork(book, dve, "experts", [dve_done])
            slot_used(dve, "bdown")
            n = dve.value_load(most[0:1, 0:1])
            with dve.If(n < CAP + 1):
                few()
                fork.end("few", [0])
            with dve.Else():
                many()
                fork.end("many", [0])
            fork.join()
            ln("B", ("ln2_g_2", "ln2_b_2"), 0, ALPHA2, lambda: None, banked=False)
            slot_used(dve, "wple")
            dve.wait_ge(h_ready.sem, h_ready.at(("h", "B")))
            for t in range(TT):
                for half in range(2):
                    b = 2 * t + half
                    bank_empty(4 + b, "pg")
                    x = hn[:, t, half * 512:half * 512 + 512]
                    v.tensor_tensor(x, x, ps[:, b, :], ALU.mult).then_inc(emptied[b].sem, 1)
                bank_empty(2 * t, "ple")
                bank_empty(2 * t + 1, "ple")
                done(v.tensor_tensor(h[:, t, :], h[:, t, :], hn[:, t, :], ALU.add), ("out", t))

        @block.gpsimd
        def _(pool):
            g = nc.gpsimd

            def done(ins, name):
                ins.then_inc(pool_done.add(name), 1)

            def link(ins):
                name = ("link", pool_done.n, tuple(pool_done.loops))
                ins.then_inc(pool_done.add(name), 1)
                pool.wait_ge(pool_done.sem, pool_done.at(name))
                plain(pool)

            def residual(tag):
                name = ("lnp", tag)
                s = slot_of[name]
                pool.wait_ge(loaded[s].sem, loaded[s].at(name))
                for t in range(TT):
                    pool.wait_ge(dve_done.sem, dve_done.at(("hn", tag, t)))
                    link(g.tensor_tensor(h[:, t, :], hn[:, t, :], ring[:, s, 0:D], ALU.mult))
                    ins = g.tensor_tensor(h[:, t, :], h[:, t, :], ring[:, s, D:2 * D], ALU.add)
                    if t == 1:
                        ins.then_inc(h_ready.add(("h", tag)), 1)
                pool.wait_ge(h_ready.sem, h_ready.at(("h", tag)))
                pool.sem_inc(used[s].sem, 1)

            pool.wait_ge(first.sem, 16 * 6)
            pool.sem_inc(h_ready.add("x"), 1)
            pool.wait_ge(dve_done.sem, dve_done.at("zeros"))
            with counted(book, pool, "L", LAYERS, [pool_done, h_ready]) as L:
                residual(0)
                up = w(UP, 516, "p (g t) -> p g t", g=2)
                tc = w(TC, T)
                pool.wait_ge(emptied[1].sem, emptied[1].at("ch", 1))
                pool.wait_ge(emptied[0].sem, emptied[0].at("cb", 1))
                plain(pool)
                link(g.tensor_copy(taps[:], cols[:, 1, bass.ds(L * 6 + 16, 6)]))
                for ct in range(2):
                    y = yT[:, ct, :]
                    link(g.tensor_scalar(y, up[:, ct, 0:T], taps[:, ct:ct + 1], None, ALU.mult))
                    for k in range(1, 3):
                        link(g.tensor_scalar(tc, up[:, ct, k:k + T], taps[:, 2 * k + ct:2 * k + ct + 1], None, ALU.mult))
                        link(g.tensor_tensor(y, y, tc, ALU.add))
                    ins = g.tensor_tensor(y, y, work[:, CC + ct * T:CC + ct * T + T], ALU.mult)
                done(ins, "conv")
                pu, sa, sbb = (w(o, 544, "p (g t) -> p g t", g=2) for o in (PU, SA, SB))
                pm = w(PM, 512, "p (g t) -> p g t", g=2)
                pool.wait_ge(emptied[1].sem, emptied[1].at("pu", 1))
                link(g.tensor_tensor(sa[:, :, 1:272], pu[:, :, 1:272], pu[:, :, 0:271], ALU.add))
                link(g.tensor_tensor(sbb[:, :, 3:272], sa[:, :, 3:272], sa[:, :, 1:270], ALU.add))

                def mean(x, lo, kt):
                    link(g.tensor_scalar(pm[lo:lo + 64, kt, :], x[lo:lo + 64, kt, 16:272], cnt[lo:lo + 64, kt, 16:17],
                                         None, ALU.mult))
                    link(g.tensor_tensor(pm[lo:lo + 64, kt, 0:16], x[lo:lo + 64, kt, 16:32], cnt[lo:lo + 64, kt, 0:16],
                                         ALU.mult))

                mean(sa, 0, 0)
                mean(sbb, 64, 0)
                link(g.tensor_tensor(sa[:, 1, 7:272], sbb[:, 1, 7:272], sbb[:, 1, 3:268], ALU.add))
                link(g.tensor_tensor(sbb[:, 1, 15:272], sa[:, 1, 15:272], sa[:, 1, 7:264], ALU.add))
                mean(sa, 0, 1)
                mean(sbb, 64, 1)
                done(g.tensor_tensor(pm, pm, pu[:, :, 16:272], ALU.subtract), "pooled")
                residual(1)
                residual(2)
                residual(3)
            pool.wait_ge(emptied[3].sem, emptied[3].at(("lru", "i", 3), 1))
            pool.wait_ge(dve_done.sem, dve_done.at("xc"))
            done(g.tensor_tensor(w(IG, 2048), w(IG, 2048), w(XC, 2048), ALU.mult), "ix")
            gob = hn[:].rearrange("p t n -> p (t n)")
            for j in range(4):
                pool.wait_ge(emptied[j % 2].sem, emptied[j % 2].at(f"mb{j}", 1))
                x = gob[:, 512 * j:512 * j + 512]
                done(g.tensor_tensor(x, x, work[:, TH + 512 * (j % 2):TH + 512 * (j % 2) + 512], ALU.mult), ("mb", j))
            residual("A")
            residual("B")


LOGIT, CHOSEN, GATES, GT, POS, IOTA, GS, GG, CMP = 0, 64, 128, 192, 448, 512, 640, 768, 1024
BUP, GGT, XG, YS, ACTS = 3072, 3584, 4096, 4608, 5120
GH, UH, SG = 6144, 7168, 8192
ACTT, MACC = 9728, 11776
GUT = ACTT

_SHAPES = {}
_INS = ['x', 'mem', 'ffn1_gate', 'ffn1_up', 'ffn1_down', 'w_in', 'conv_w', 'rec_lb', 'rec_norm_g', 'pool_w',
        'pool_scale', 'w_out', 'ca_q', 'ca_k', 'ca_v', 'ca_o', 'ffn2_gate', 'ffn2_up', 'ffn2_down', 'ln_g', 'ln_b',
        'p_2', 'w_in_2', 'conv_w_2', 'conv_b_2', 'lru_w_r_2', 'lru_b_r_2', 'lru_w_i_2', 'lru_b_i_2', 'lru_lambda_2',
        'gla_w_gate_2', 'gla_b_gate_2', 'gla_norm_g_2', 'w_out_2', 'ln1_g_2', 'ln1_b_2', 'w_router_2', 'b_router_2',
        'w_up_2', 'b_up_2', 'w_down_2', 'b_down_2', 'ln2_g_2', 'ln2_b_2', 'w_ple_2', 'w_ple_gate_2', 'b_ple_gate_2']


def constants():
    s, t = np.arange(P)[:, None], np.arange(P)[None, :]
    apart = s ^ t
    mask = np.zeros((P, 8, P), np.float32)
    mask[:, 0] = s == t
    for lv in range(1, 8):
        mask[:, lv] = (t > s) & (apart >> (lv - 1) == 1)
    window = np.array([[2, 8], [4, 16]])[np.arange(P) // 64]
    count = np.minimum(np.arange(17) + 1, window[:, :, None])
    count[:, :, 16] = window
    tri = np.broadcast_to((np.arange(32)[None, :] < np.arange(32)[:, None]).reshape(1, 1024), (P, 1024))
    return {"c_ident": np.eye(P, dtype=np.float32), "c_mask": mask,
            "c_moe": np.stack([(s < t).astype(np.float32), np.broadcast_to((t % CAP).astype(np.float32), (P, P))], 1),
            "c_cnt": (1.0 / count).astype(np.float32), "c_tri": np.ascontiguousarray(tri, dtype=np.float32)}


def kernel(**inputs):
    import concourse.bacc as _bacc
    from concourse.bass_utils import run_bass_kernel_spmd as _run

    arrays = {n: np.ascontiguousarray(inputs[n]) for n in _INS}
    arrays.update(constants())
    book = Book()
    for _ in range(2):
        nc = _bacc.Bacc("TRN2", target_bir_lowering=False, num_devices=1)
        a = {n: nc.dram_tensor(f"in_{n}_dram", v.shape, mybir.dt.from_np(v.dtype), kind="ExternalInput").ap()
             for n, v in arrays.items()}
        a["out"] = nc.dram_tensor("out_0_dram", (1, T, D), F32, kind="ExternalOutput").ap()
        program(nc, book, a)
        book.turn()
    r = _run(nc, [{f"in_{n}_dram": v for n, v in arrays.items()}], core_ids=[0])
    return r.results[0]["out_0_dram"]
```
